# Optimizing a Trainium2 kernel written in Bass

```python
import jax
import jax.numpy as jnp
from jax import lax
import numpy as np

D_MODEL = 1024
BATCH = 1
SEQ = 256
DEPTH = 2

GRID_W = 64
CTX_LEN = 256
HEAD_DIM = 64
BLOCK = 128
WINDOW = 128
ROPE_BASE = 10000.0
NORM_EPS = 1e-6
NEG_INF = -1e30

N_BRANCH = 4
BRANCH_WIDTH = 256

RW_HEADS = 4
RW_WIDTH = RW_HEADS * HEAD_DIM
RW_DECAY_LORA = 64
RW_AAA_LORA = 64
RW_MV_LORA = 32
RW_GATE_LORA = 128
RW_GN_EPS = 64e-5

SW_HEADS = 4
SW_KV_HEADS = 2

MLA_HEADS = 4
MLA_NOPE = 64
MLA_ROPE = 32
MLA_V = 64
MLA_Q_RANK = 256
MLA_KV_RANK = 128

GA_HEADS = 4
GA_KV_HEADS = 2

D_FF = 3584
N_EXPERTS = 8
TOP_K = 2
D_FF_EXPERT = 3584
MOE_BLOCK = 128

IN_WIDTHS = (4 * RW_WIDTH,
             SW_HEADS * HEAD_DIM, SW_KV_HEADS * HEAD_DIM, SW_KV_HEADS * HEAD_DIM,
             MLA_Q_RANK, MLA_KV_RANK, MLA_ROPE,
             GA_HEADS * HEAD_DIM, GA_KV_HEADS * HEAD_DIM, GA_KV_HEADS * HEAD_DIM,
             N_BRANCH * D_MODEL)
IN_WIDTH = (4 * RW_WIDTH + (SW_HEADS + 2 * SW_KV_HEADS) * HEAD_DIM
            + MLA_Q_RANK + MLA_KV_RANK + MLA_ROPE
            + (GA_HEADS + 2 * GA_KV_HEADS) * HEAD_DIM + N_BRANCH * D_MODEL)

kernel_name = 'hybrid_flow_backbone'

def rms_norm(x, g):
    xf = x.astype(jnp.float32)
    y = xf * lax.rsqrt(jnp.mean(xf * xf, axis=-1, keepdims=True) + NORM_EPS)
    return (y * g.astype(jnp.float32)).astype(x.dtype)

def split_cols(p, widths):
    out, off = [], 0
    for w in widths:
        out.append(p[..., off:off + w])
        off += w
    return out

def axial_rope_tables(n_tokens, rot_dim):
    rows = n_tokens // GRID_W
    row = jnp.repeat(jnp.arange(rows, dtype=jnp.float32), GRID_W)
    col = jnp.tile(jnp.arange(GRID_W, dtype=jnp.float32), rows)
    n_freq = rot_dim // 4
    inv_freq = ROPE_BASE ** (-jnp.arange(n_freq, dtype=jnp.float32) / n_freq)
    ang = jnp.concatenate([row[:, None] * inv_freq, col[:, None] * inv_freq], axis=-1)
    return jnp.cos(ang), jnp.sin(ang)

def apply_rope(x, cos, sin):
    half = x.shape[-1] // 2
    c = cos[None, :, None, :].astype(x.dtype)
    s = sin[None, :, None, :].astype(x.dtype)
    x1, x2 = x[..., :half], x[..., half:]
    return jnp.concatenate([x1 * c - x2 * s, x1 * s + x2 * c], axis=-1)

def context_attention(q, k, v, scale, sink=None):
    b, n = q.shape[:2]
    s = jnp.einsum('bqhgd,bkhd->bhgqk', q, k).astype(jnp.float32) * scale
    if sink is not None:
        s_sink = jnp.broadcast_to(sink[None, :, :, None, None].astype(jnp.float32), s.shape[:-1] + (1,))
        p = jax.nn.softmax(jnp.concatenate([s_sink, s], axis=-1), axis=-1)[..., 1:]
    else:
        p = jax.nn.softmax(s, axis=-1)
    o = jnp.einsum('bhgqk,bkhd->bqhgd', p.astype(v.dtype), v)
    return o.reshape(b, n, -1)

def banded_window_attention(q, k, v, k_ctx, v_ctx, sink, scale):
    b, s_len, hk, g, d = q.shape
    nb = s_len // BLOCK
    qb = q.reshape(b, nb, BLOCK, hk, g, d)

    def neighbours(t):
        tb = jnp.pad(t.reshape(b, nb, BLOCK, hk, t.shape[-1]), ((0, 0), (1, 1), (0, 0), (0, 0), (0, 0)))
        return jnp.concatenate([tb[:, :-2], tb[:, 1:-1], tb[:, 2:]], axis=2)

    kb, vb = neighbours(k), neighbours(v)
    blk = jnp.arange(nb)
    q_pos = blk[:, None] * BLOCK + jnp.arange(BLOCK)[None, :]
    k_pos = (blk[:, None] - 1) * BLOCK + jnp.arange(3 * BLOCK)[None, :]
    valid = ((jnp.abs(q_pos[:, :, None] - k_pos[:, None, :]) <= WINDOW)
             & (k_pos >= 0)[:, None, :] & (k_pos < s_len)[:, None, :])
    s_win = jnp.einsum('bnqhgd,bnkhd->bnhgqk', qb, kb).astype(jnp.float32) * scale
    s_win = jnp.where(valid[None, :, None, None], s_win, NEG_INF)
    s_ctx = jnp.einsum('bnqhgd,bchd->bnhgqc', qb, k_ctx).astype(jnp.float32) * scale
    s_sink = jnp.broadcast_to(sink[None, None, :, :, None, None].astype(jnp.float32), s_ctx.shape[:-1] + (1,))
    p = jax.nn.softmax(jnp.concatenate([s_sink, s_ctx, s_win], axis=-1), axis=-1).astype(v.dtype)
    n_ctx = k_ctx.shape[1]
    o = (jnp.einsum('bnhgqc,bchd->bnqhgd', p[..., 1:1 + n_ctx], v_ctx)
         + jnp.einsum('bnhgqk,bnkhd->bnqhgd', p[..., 1 + n_ctx:], vb))
    return o.reshape(b, s_len, -1)

def dense_block_attention(q, k, v, scale):
    b, s_len, hk, g, dq = q.shape
    nb = s_len // BLOCK
    qb = jnp.moveaxis(q.reshape(b, nb, BLOCK, hk, g, dq), 1, 0)

    def one_block(qblk):
        s = jnp.einsum('bqhgd,bkhd->bhgqk', qblk, k).astype(jnp.float32) * scale
        p = jax.nn.softmax(s, axis=-1).astype(v.dtype)
        return jnp.einsum('bhgqk,bkhd->bqhgd', p, v)

    o = lax.map(one_block, qb)
    return jnp.moveaxis(o, 0, 1).reshape(b, s_len, -1)

def gqa_heads(q, k, v, n_heads, n_kv, rope=None, q_gain=None, k_gain=None):
    b, n, _ = q.shape
    q = q.reshape(b, n, n_heads, HEAD_DIM)
    k = k.reshape(b, n, n_kv, HEAD_DIM)
    v = v.reshape(b, n, n_kv, HEAD_DIM)
    if q_gain is not None:
        q = rms_norm(q, q_gain)
        k = rms_norm(k, k_gain)
    if rope is not None:
        q = apply_rope(q, rope[0], rope[1])
        k = apply_rope(k, rope[0], rope[1])
    return q.reshape(b, n, n_kv, n_heads // n_kv, HEAD_DIM), k, v

def window_mixer(pc, pl, sink, rope, ctx_out):
    scale = HEAD_DIM ** -0.5
    qc, kc, vc = gqa_heads(pc[0], pc[1], pc[2], SW_HEADS, SW_KV_HEADS)
    ql, kl, vl = gqa_heads(pl[0], pl[1], pl[2], SW_HEADS, SW_KV_HEADS, rope)
    sink = sink.reshape(SW_KV_HEADS, SW_HEADS // SW_KV_HEADS)
    y_lat = banded_window_attention(ql, kl, vl, kc, vc, sink, scale)
    y_ctx = context_attention(qc, kc, vc, scale, sink) if ctx_out else None
    return y_ctx, y_lat

def grid_attention_mixer(pc, pl, q_gain, k_gain, rope, ctx_out):
    scale = HEAD_DIM ** -0.5
    qc, kc, vc = gqa_heads(pc[0], pc[1], pc[2], GA_HEADS, GA_KV_HEADS, None, q_gain, k_gain)
    ql, kl, vl = gqa_heads(pl[0], pl[1], pl[2], GA_HEADS, GA_KV_HEADS, rope, q_gain, k_gain)
    y_lat = dense_block_attention(ql, jnp.concatenate([kc, kl], axis=1), jnp.concatenate([vc, vl], axis=1), scale)
    y_ctx = context_attention(qc, kc, vc, scale) if ctx_out else None
    return y_ctx, y_lat

def mla_mixer(pc, pl, q_gain, w_uq, kv_gain, w_ukv, rope, ctx_out):
    scale = (MLA_NOPE + MLA_ROPE) ** -0.5

    def project(cq, ckv, k_rope, rope_tab):
        b, n, _ = cq.shape
        q = (rms_norm(cq, q_gain) @ w_uq).reshape(b, n, MLA_HEADS, MLA_NOPE + MLA_ROPE)
        kv = (rms_norm(ckv, kv_gain) @ w_ukv).reshape(b, n, MLA_HEADS, MLA_NOPE + MLA_V)
        q_nope, q_pe = q[..., :MLA_NOPE], q[..., MLA_NOPE:]
        k_nope, v = kv[..., :MLA_NOPE], kv[..., MLA_NOPE:]
        k_pe = k_rope[:, :, None, :]
        if rope_tab is not None:
            q_pe = apply_rope(q_pe, rope_tab[0], rope_tab[1])
            k_pe = apply_rope(k_pe, rope_tab[0], rope_tab[1])
        q = jnp.concatenate([q_nope, q_pe], axis=-1)
        k = jnp.concatenate([k_nope, jnp.broadcast_to(k_pe, (b, n, MLA_HEADS, MLA_ROPE))], axis=-1)
        return q[:, :, :, None, :], k, v

    qc, kc, vc = project(pc[0], pc[1], pc[2], None)
    ql, kl, vl = project(pl[0], pl[1], pl[2], rope)
    y_lat = dense_block_attention(ql, jnp.concatenate([kc, kl], axis=1), jnp.concatenate([vc, vl], axis=1), scale)
    y_ctx = context_attention(qc, kc, vc, scale) if ctx_out else None
    return y_ctx, y_lat

def centred_token_shift(f, mu):
    prev = jnp.pad(f[:, :-1], ((0, 0), (1, 0), (0, 0)))
    nxt = jnp.pad(f[:, 1:], ((0, 0), (0, 1), (0, 0)))
    return f + mu[0] * (prev - f) + mu[1] * (nxt - f)

def rwkv7_scan(r, decay, k, v, a, b, state0, reverse):
    xs = tuple(jnp.moveaxis(t.astype(jnp.float32), 1, 0) for t in (r, decay, k, v, a, b))

    def step(state, inp):
        r_t, w_t, k_t, v_t, a_t, b_t = inp
        sa = jnp.einsum('bhvk,bhk->bhv', state, a_t)
        state = (state * w_t[:, :, None, :] + sa[..., None] * b_t[:, :, None, :]
                 + v_t[..., None] * k_t[:, :, None, :])
        return state, jnp.einsum('bhvk,bhk->bhv', state, r_t)

    final, y = lax.scan(step, state0, xs, reverse=reverse)
    return final, jnp.moveaxis(y, 0, 1)

def rwkv7_mixer(f_ctx, f_lat, vf_ctx, vf_lat, rw, ctx_out):
    def heads(t):
        return t.reshape(t.shape[:-1] + (RW_HEADS, HEAD_DIM))

    r_k = rw['r_k'].reshape(RW_HEADS, HEAD_DIM)

    def features(f, vf):
        f = centred_token_shift(f, rw['mu'])
        r, k, v, z = jnp.split(f, 4, axis=-1)
        if vf is None:
            vf = v
        else:
            v = v + (vf - v) * jax.nn.sigmoid(rw['v0'] + (z @ rw['v1']) @ rw['v2'])
        kk = heads(k * rw['k_k']).astype(jnp.float32)
        kk = (kk * lax.rsqrt(jnp.sum(kk * kk, axis=-1, keepdims=True) + 1e-12)).astype(f.dtype)
        g = jax.nn.sigmoid(z @ rw['g1']) @ rw['g2']
        per_dir = []
        for d in range(2):
            w = -jax.nn.softplus(-(rw['w0'][d] + jnp.tanh(z @ rw['w1'][d]) @ rw['w2'][d])) - 0.5
            decay = jnp.exp(-jnp.exp(w.astype(jnp.float32)))
            a = jax.nn.sigmoid(rw['a0'][d] + (z @ rw['a1'][d]) @ rw['a2'][d])
            k_d = k * (1 + (a - 1) * rw['k_a'])
            per_dir.append((heads(decay), heads(a), heads(k_d)))
        return heads(r), heads(v), kk, g, per_dir, vf

    r_c, v_c, kk_c, g_c, dir_c, vf_ctx = features(f_ctx, vf_ctx)
    r_l, v_l, kk_l, g_l, dir_l, vf_lat = features(f_lat, vf_lat)
    state0 = jnp.zeros((f_lat.shape[0], RW_HEADS, HEAD_DIM, HEAD_DIM), jnp.float32)
    y_c, y_l, bonus_c, bonus_l = 0.0, 0.0, 0.0, 0.0
    for d in range(2):
        rev = d == 1
        dec, a, k_d = dir_c[d]
        s_ctx, y = rwkv7_scan(r_c, dec, k_d, v_c, -kk_c, kk_c * a, state0, rev)
        if ctx_out:
            y_c = y_c + y
            bonus_c = bonus_c + jnp.sum(r_c * k_d * r_k, axis=-1, keepdims=True) * v_c
        dec, a, k_d = dir_l[d]
        _, y = rwkv7_scan(r_l, dec, k_d, v_l, -kk_l, kk_l * a, s_ctx, rev)
        y_l = y_l + y
        bonus_l = bonus_l + jnp.sum(r_l * k_d * r_k, axis=-1, keepdims=True) * v_l

    ln_w = rw['ln_w'].reshape(RW_HEADS, HEAD_DIM).astype(jnp.float32)
    ln_b = rw['ln_b'].reshape(RW_HEADS, HEAD_DIM).astype(jnp.float32)

    def finish(y, bonus, g):
        mu = jnp.mean(y, axis=-1, keepdims=True)
        var = jnp.mean(jnp.square(y - mu), axis=-1, keepdims=True)
        yn = (y - mu) * lax.rsqrt(var + RW_GN_EPS) * ln_w + ln_b
        o = yn.astype(g.dtype) + bonus
        return o.reshape(g.shape) * g

    y_lat = finish(y_l, bonus_l, g_l)
    y_ctx = finish(y_c, bonus_c, g_c) if ctx_out else None
    return y_ctx, y_lat, vf_ctx, vf_lat

def hybrid_token_mixer(h_ctx, h_lat, vf_ctx, vf_lat, w_in, w_branch, w_out, rw, sw_sink,
                       mla_q_norm, mla_w_uq, mla_kv_norm, mla_w_ukv, ga_q_norm, ga_k_norm,
                       rope64, rope32, ctx_out):
    pc = split_cols(h_ctx @ w_in, IN_WIDTHS)
    pl = split_cols(h_lat @ w_in, IN_WIDTHS)
    ya_c, ya_l, vf_ctx, vf_lat = rwkv7_mixer(pc[0], pl[0], vf_ctx, vf_lat, rw, ctx_out)
    yb_c, yb_l = window_mixer(pc[1:4], pl[1:4], sw_sink, rope64, ctx_out)
    yc_c, yc_l = mla_mixer(pc[4:7], pl[4:7], mla_q_norm, mla_w_uq, mla_kv_norm, mla_w_ukv, rope32, ctx_out)
    yd_c, yd_l = grid_attention_mixer(pc[7:10], pl[7:10], ga_q_norm, ga_k_norm, rope64, ctx_out)

    def merge(ys, gate_cols):
        gates = jax.nn.sigmoid(gate_cols.astype(jnp.float32)).astype(gate_cols.dtype)
        m = None
        for i, y in enumerate(ys):
            term = gates[..., i * D_MODEL:(i + 1) * D_MODEL] * (y @ w_branch[i])
            m = term if m is None else m + term
        return m @ w_out

    out_lat = merge([ya_l, yb_l, yc_l, yd_l], pl[10])
    out_ctx = merge([ya_c, yb_c, yc_c, yd_c], pc[10]) if ctx_out else None
    return out_ctx, out_lat, vf_ctx, vf_lat

def swiglu(h, w1, w3, w2):
    return (jax.nn.silu(h @ w1) * (h @ w3)) @ w2

def moe_swiglu(h, w_router, w1, w3, w2):
    n_tok, d = h.shape
    logits = (h @ w_router).astype(jnp.float32)
    top_logit, top_idx = lax.top_k(logits, TOP_K)
    gates = jax.nn.softmax(top_logit, axis=-1)
    n_assign = n_tok * TOP_K
    flat_e = top_idx.reshape(-1)
    order = jnp.argsort(flat_e)
    sorted_e = flat_e[order]
    sorted_tok = (order // TOP_K).astype(jnp.int32)
    sorted_gate = gates.reshape(-1)[order]
    counts = jnp.bincount(flat_e, length=N_EXPERTS)
    padded = (counts + MOE_BLOCK - 1) // MOE_BLOCK * MOE_BLOCK
    start = jnp.cumsum(counts) - counts
    pend = jnp.cumsum(padded)
    pstart = pend - padded
    dest = pstart[sorted_e] + jnp.arange(n_assign) - start[sorted_e]
    n_blocks = -(-n_assign // MOE_BLOCK) + N_EXPERTS
    n_rows = n_blocks * MOE_BLOCK
    tok = jnp.zeros((n_rows,), jnp.int32).at[dest].set(sorted_tok)
    gate = jnp.zeros((n_rows,), h.dtype).at[dest].set(sorted_gate.astype(h.dtype))
    block_e = jnp.minimum(jnp.searchsorted(pend, jnp.arange(n_blocks) * MOE_BLOCK, side='right'), N_EXPERTS - 1)
    xb = h[tok].reshape(n_blocks, MOE_BLOCK, d)

    def expert_block(args):
        xblk, e = args
        return (jax.nn.silu(xblk @ w1[e]) * (xblk @ w3[e])) @ w2[e]

    yb = lax.map(expert_block, (xb, block_e)).reshape(n_rows, d)
    return jnp.zeros_like(h).at[tok].add(yb * gate[:, None])

def setup_inputs(seed: int = 0) -> dict:
    key = jax.random.key(seed)
    keys = iter(jax.random.split(key, 64))
    f32 = jnp.float32

    def normal(shape, scale=1.0):
        return jax.random.normal(next(keys), shape, f32) * scale

    def gain(shape):
        return 1.0 + normal(shape, 0.05)

    L, D, W = DEPTH, D_MODEL, RW_WIDTH
    n_dense, n_moe = (DEPTH + 1) // 2, DEPTH // 2
    return {
        'x': normal((BATCH, SEQ, D)),
        'c': normal((BATCH, D)),
        'ctx': normal((BATCH, CTX_LEN, D)),
        'c_ctx': normal((D,)),
        'w_mod': normal((L, D, 6 * D), 0.02),
        'b_mod': normal((L, 6 * D), 0.02),
        'norm1': gain((L, D)),
        'norm2': gain((L, D)),
        'w_in': normal((L, D, IN_WIDTH), D ** -0.5),
        'w_branch': normal((L, N_BRANCH, BRANCH_WIDTH, D), BRANCH_WIDTH ** -0.5),
        'w_out': normal((L, D, D), D ** -0.5),
        'rw_mu': jax.random.uniform(next(keys), (L, 2, 4 * W), f32, 0.0, 0.5),
        'rw_w0': jnp.linspace(-6.0, -1.0, W, dtype=f32)[None, None, :] + normal((L, 2, W), 0.1),
        'rw_w1': normal((L, 2, W, RW_DECAY_LORA), W ** -0.5),
        'rw_w2': normal((L, 2, RW_DECAY_LORA, W), 0.3 * RW_DECAY_LORA ** -0.5),
        'rw_a0': normal((L, 2, W), 0.1),
        'rw_a1': normal((L, 2, W, RW_AAA_LORA), W ** -0.5),
        'rw_a2': normal((L, 2, RW_AAA_LORA, W), 0.5 * RW_AAA_LORA ** -0.5),
        'rw_v0': normal((L - 1, W), 0.3),
        'rw_v1': normal((L - 1, W, RW_MV_LORA), W ** -0.5),
        'rw_v2': normal((L - 1, RW_MV_LORA, W), 0.5 * RW_MV_LORA ** -0.5),
        'rw_g1': normal((L, W, RW_GATE_LORA), W ** -0.5),
        'rw_g2': normal((L, RW_GATE_LORA, W), RW_GATE_LORA ** -0.5),
        'rw_k_k': 0.85 + normal((L, W), 0.05),
        'rw_k_a': gain((L, W)),
        'rw_r_k': normal((L, W), 0.1),
        'rw_ln_w': gain((L, W)),
        'rw_ln_b': normal((L, W), 0.02),
        'sw_sink': normal((L, SW_HEADS), 0.5),
        'mla_q_norm': gain((L, MLA_Q_RANK)),
        'mla_w_uq': normal((L, MLA_Q_RANK, MLA_HEADS * (MLA_NOPE + MLA_ROPE)), MLA_Q_RANK ** -0.5),
        'mla_kv_norm': gain((L, MLA_KV_RANK)),
        'mla_w_ukv': normal((L, MLA_KV_RANK, MLA_HEADS * (MLA_NOPE + MLA_V)), MLA_KV_RANK ** -0.5),
        'ga_q_norm': gain((L, HEAD_DIM)),
        'ga_k_norm': gain((L, HEAD_DIM)),
        'ffn_w1': normal((n_dense, D, D_FF), D ** -0.5),
        'ffn_w3': normal((n_dense, D, D_FF), D ** -0.5),
        'ffn_w2': normal((n_dense, D_FF, D), D_FF ** -0.5),
        'moe_router': normal((n_moe, D, N_EXPERTS), D ** -0.5),
        'moe_w1': normal((n_moe, N_EXPERTS, D, D_FF_EXPERT), D ** -0.5),
        'moe_w3': normal((n_moe, N_EXPERTS, D, D_FF_EXPERT), D ** -0.5),
        'moe_w2': normal((n_moe, N_EXPERTS, D_FF_EXPERT, D), D_FF_EXPERT ** -0.5),
        'final_norm': gain((D,)),
    }

def reference(x, c, ctx, c_ctx, w_mod, b_mod, norm1, norm2, w_in, w_branch, w_out,
              rw_mu, rw_w0, rw_w1, rw_w2, rw_a0, rw_a1, rw_a2, rw_v0, rw_v1, rw_v2,
              rw_g1, rw_g2, rw_k_k, rw_k_a, rw_r_k, rw_ln_w, rw_ln_b, sw_sink,
              mla_q_norm, mla_w_uq, mla_kv_norm, mla_w_ukv, ga_q_norm, ga_k_norm,
              ffn_w1, ffn_w3, ffn_w2, moe_router, moe_w1, moe_w3, moe_w2, final_norm):
    b, s_len, d = x.shape
    n_ctx_tok = ctx.shape[1]
    rope64 = axial_rope_tables(s_len, HEAD_DIM)
    rope32 = axial_rope_tables(s_len, MLA_ROPE)
    silu_c = jax.nn.silu(c)
    silu_cc = jax.nn.silu(c_ctx)
    x_lat, x_ctx = x, ctx
    vf_lat, vf_ctx = None, None
    for l in range(DEPTH):
        ctx_out = l < DEPTH - 1
        mod_l = silu_c @ w_mod[l] + b_mod[l]
        mod_c = silu_cc @ w_mod[l] + b_mod[l]
        sh1, sc1, g1, sh2, sc2, g2 = jnp.split(mod_l[:, None, :], 6, axis=-1)
        csh1, csc1, cg1, csh2, csc2, cg2 = jnp.split(mod_c, 6, axis=-1)

        h_lat = rms_norm(x_lat, norm1[l]) * (1 + sc1) + sh1
        h_ctx = rms_norm(x_ctx, norm1[l]) * (1 + csc1) + csh1
        rw = dict(mu=rw_mu[l], w0=rw_w0[l], w1=rw_w1[l], w2=rw_w2[l],
                  a0=rw_a0[l], a1=rw_a1[l], a2=rw_a2[l],
                  v0=rw_v0[l - 1] if l > 0 else None,
                  v1=rw_v1[l - 1] if l > 0 else None,
                  v2=rw_v2[l - 1] if l > 0 else None,
                  g1=rw_g1[l], g2=rw_g2[l], k_k=rw_k_k[l], k_a=rw_k_a[l], r_k=rw_r_k[l],
                  ln_w=rw_ln_w[l], ln_b=rw_ln_b[l])
        out_ctx, out_lat, vf_ctx, vf_lat = hybrid_token_mixer(
            h_ctx, h_lat, vf_ctx, vf_lat, w_in[l], w_branch[l], w_out[l], rw, sw_sink[l],
            mla_q_norm[l], mla_w_uq[l], mla_kv_norm[l], mla_w_ukv[l], ga_q_norm[l], ga_k_norm[l],
            rope64, rope32, ctx_out)
        x_lat = x_lat + g1 * out_lat

        f_lat = rms_norm(x_lat, norm2[l]) * (1 + sc2) + sh2
        if ctx_out:
            x_ctx = x_ctx + cg1 * out_ctx
            f_ctx = rms_norm(x_ctx, norm2[l]) * (1 + csc2) + csh2
            tokens = jnp.concatenate([f_ctx.reshape(-1, d), f_lat.reshape(-1, d)], axis=0)
            n_c = b * n_ctx_tok
        else:
            tokens = f_lat.reshape(-1, d)
            n_c = 0
        if l % 2 == 0:
            ffn_out = swiglu(tokens, ffn_w1[l // 2], ffn_w3[l // 2], ffn_w2[l // 2])
        else:
            ffn_out = moe_swiglu(tokens, moe_router[l // 2], moe_w1[l // 2], moe_w3[l // 2], moe_w2[l // 2])
        x_lat = x_lat + g2 * ffn_out[n_c:].reshape(b, s_len, d)
        if ctx_out:
            x_ctx = x_ctx + cg2 * ffn_out[:n_c].reshape(b, n_ctx_tok, d)
    return rms_norm(x_lat, final_norm)


_drawn_inputs = setup_inputs


def setup_inputs(seed=0):
    import zlib

    import numpy as np

    out = dict(_drawn_inputs(seed))
    spreads = {}
    factors = {'norm1': 3.143,
     'rw_w1': 3.777,
     'rw_w2': 6.002,
     'rw_a0': 4.879,
     'rw_v0': 2.826,
     'rw_ln_w': 5.566,
     'rw_ln_b': 7.713,
     'sw_sink': 64.0,
     'mla_q_norm': 8.0,
     'mla_kv_norm': 7.877,
     'ga_q_norm': 8.0,
     'ga_k_norm': 8.0}
    for name, (base, spread) in spreads.items():
        noise = np.random.default_rng([zlib.crc32(name.encode()), seed]).standard_normal(out[name].shape)
        drawn = base * np.exp(spread * noise) if base else spread * noise
        out[name] = jnp.asarray(drawn.astype(out[name].dtype))
    for name, factor in factors.items():
        out[name] = (out[name] * factor).astype(out[name].dtype)
    return out
```

```python
import numpy as np
import concourse.bass as bass
from concourse import mybir
from contextlib import ExitStack

P = 128
D = 1024
KD = D // P
CTX = 256
LAT = 256
TOK = CTX + LAT
DEPTH = 2
UW = 2048
UC = UW // KD
RING = 6
CH = 128
NCH = TOK // CH
HD = 64
EXPERTS = 8
FF = 3584
FT = FF // P
PAIRS = FF // UC
SLOTS = 128
MOE_UNITS = 3 * PAIRS
MOD_UNITS = 6 * D // UC
NEG = -1e30
F32 = mybir.dt.float32
I32 = mybir.dt.int32
F32R = mybir.dt.float32r

VEC = {}
_n = 0
for _name, _w in (("c", 8), ("cc", 8), ("b_mod", 96), ("norm1", 16), ("norm2", 16), ("final", 8), ("mu", 32),
                  ("w0", 8), ("a0", 8), ("v0", 2), ("k_k", 4), ("k_a", 4), ("r_k", 4), ("ln_w", 4), ("ln_b", 4),
                  ("mla_q", 4), ("mla_kv", 2), ("ga_q", 2), ("ga_k", 2), ("sink", 8), ("eps", 1), ("eps_kk", 1),
                  ("eps_gn", 1)):
    VEC[_name] = _n
    _n += _w
NVEC = _n

SM = {}
_n = 0
for _name, _w in (("w1", 256), ("a1", 256), ("g1", 256), ("v1", 64), ("w2", 256), ("a2", 256), ("g2", 256),
                  ("v2", 256), ("uq", 768), ("ukv", 512)):
    SM[_name] = _n
    _n += _w
NSM = _n

CN = {}
_n = 0
for _name, _w in (("ident", 128), ("ones", 128), ("heads", 128), ("rot64", 128), ("rot96", 128), ("tri", 128),
                  ("cos64", 256), ("sin64", 256), ("cos96", 256), ("sin96", 256), ("band", 512),
                  ("strict0", 128), ("strict1", 128), ("incl0", 128), ("incl1", 128),
                  ("near0", 128), ("near1", 128), ("far0", 128), ("far1", 128), ("iota", 256), ("lane8", 8)):
    CN[_name] = _n
    _n += _w
NCN = _n

PROJ_UNITS, MERGE_UNITS, OUT_UNITS = 10, 20, 4
FFN_IN_UNITS, FFN_OUT_UNITS = 2 * PAIRS, 16
DENSE_UNITS = 2 * MOD_UNITS + 2 * (PROJ_UNITS + MERGE_UNITS + OUT_UNITS) + FFN_IN_UNITS + FFN_OUT_UNITS
ALL_UNITS = DENSE_UNITS + EXPERTS * MOE_UNITS
assert MOE_UNITS % RING == 0

NT = 44
R_, K_, V_, Z_ = 8, 10, 12, 14
KK_, G_, KS_, TMP_ = 0, 2, 4, 6
TH_, AH_, GH_, VH_ = 16, 17, 18, 19
LW_, Q_, A_, KDIR_ = 20, 22, 24, 26
AR_, BH_, KH_ = 28, 32, 34
Y_, VT_ = 18, 14
M_ = 36
SWQ, SWK, SWV, CQ, CKV, KPE, GAQ, GAK, GAV = 8, 10, 11, 12, 14, 15, 16, 18, 19
QC, KC, VC, PB, PTB, SB = 20, 24, 28, 30, 34, 36
SCR = 36
ROWS = 43
MT, SG, MTMP = 20, 30, 38
NSQ, NR = 30, 38


class Shifted:

    def __init__(self, ap):
        self.ap = ap

    def __getitem__(self, key):
        rows, cols = key
        return self.ap[rows, cols.start - CTX:cols.stop - CTX]


class Book:

    def __init__(self, known):
        self.known, self.marks, self.count, self.known_next = known, {}, {}, {}

    def tick(self, sem, *step):
        self.count[sem.name] = self.count.get(sem.name, 0) + 1
        self.marks[step] = (sem.name, self.count[sem.name])
        return sem, 1

    def again(self, sem):
        self.count[sem.name] = 0

    def reached(self, sem):
        return self.count.get(sem.name, 0)


def backbone(nc, wstream, small, vecs, consts, router, xin, out, known):
    book = Book(known)
    ALU, ACT, AX = mybir.AluOpType, mybir.ActivationFunctionType, mybir.AxisListType
    ctx = ExitStack()
    with ctx:
        def sb(name, shape, dt=F32):
            return ctx.enter_context(nc.sbuf_tensor(name, shape, dt))

        def sem(name):
            return ctx.enter_context(nc.semaphore(name))

        ring = sb("ring", [P, RING, UW])
        xT = sb("xT", [P, KD, TOK])
        hT_at = nc.sbuf_base
        hT = sb("hT", [P, KD, TOK])
        arena_at = nc.sbuf_base
        arena = sb("arena", [P, NT, TOK])
        vfirst = sb("vfirst", [P, 2, TOK])
        sm = sb("sm", [P, NSM])
        vec = sb("vec", [P, NVEC])
        cn = sb("cn", [P, NCN])
        csil = sb("csil", [P, KD, 2])
        modT = sb("modT", [P, DEPTH, 48, 2])
        gain = sb("gain", [P, DEPTH, 2, KD, 2])
        mu0 = sb("mu0", [P, KD])
        omka = sb("omka", [P, 2])
        half = sb("half", [P, 2, NCH])
        edec = sb("edec", [P, 2, NCH])
        scl = sb("scl", [P, 2])
        state = sb("state", [P, 2, HD])
        u0 = sb("u0", [P, 2, 2, HD])
        u1 = sb("u1", [P, 2, 2, HD])
        uu = sb("uu", [P, 2, 2, HD])
        mx = sb("mx", [P, 4])
        nm = sb("nm", [P, 4])
        dn = sb("dn", [P, 4])
        es = sb("es", [P, 4])
        rs = sb("rs", [P, 4])
        bank = [ctx.enter_context(nc.psum_tensor(f"bank{i}", [P, TOK], F32)) for i in range(8)]

        unit_loaded = [sem(f"unit_loaded{i}") for i in range(RING)]
        unit_used = sem("unit_used")
        x_loaded, vec_loaded, const_loaded = sem("x_loaded"), sem("vec_loaded"), sem("const_loaded")
        small_loaded, router_loaded, out_stored = sem("small_loaded"), sem("router_loaded"), sem("out_stored")
        products = sem("products")
        vectors = sem("vectors")
        scalars = sem("scalars")
        pooled = sem("pooled")
        tick = book.tick
        by_name = {s.name: s for s in (unit_used, products, vectors, scalars, pooled)}

        def done(*step):
            name, value = book.known.get(step, ("products", 1))
            return by_name[name], value

        def T(i, n=1):
            return arena[:, i, :] if n == 1 else arena[:, i:i + n, :]

        def V(name, i=0, n=1):
            return vec[:, VEC[name] + i:VEC[name] + i + n]

        def C(name, n=128, at=0):
            return cn[:, CN[name] + at:CN[name] + at + n]

        def S(name, at=0, n=128):
            return sm[:, SM[name] + at:SM[name] + at + n]

        def rows(h):
            return slice(HD * (h % 2), HD * (h % 2) + HD)

        ar = T(AR_, 4).rearrange("p a b -> p (a b)").rearrange("p (j c s t) -> p j c s t", j=2, c=NCH, s=2)
        vt = T(VT_, 2).rearrange("p a b -> p (a b)").rearrange("p (c f) -> p c f", c=NCH)

        def half_tiles(i):
            return T(i, 2).rearrange("p a (k h t) -> p a k h t", k=2, h=2)
        DD = half_tiles(M_)
        D2 = half_tiles(M_ + 2)
        AR2 = half_tiles(M_ + 4)
        EA = half_tiles(A_)
        FG = half_tiles(M_ + 6)
        D8 = T(KDIR_).rearrange("p (a h t) -> p a h t", a=2, h=2)
        bk = T(TMP_)

        ORDER = {0: (0, 1, 2, 3), 1: (1, 0, 3, 2)}
        groups = [(d, c) for d in range(2) for c in ORDER[d]]

        def q_blocks(l):
            lat = [(CTX, TOK), (CTX + P, TOK)]
            return lat if l == DEPTH - 1 else lat + [(0, CTX), (P, CTX)]

        def heads_of(l):
            return [(br, h, q, nk) for br in range(3) for h in range(4) for q, nk in q_blocks(l)]
        rope_jobs = [("swq", 0), ("swq", 1), ("swk", 0), ("gaq", 0), ("gaq", 1), ("gak", 0),
                     ("qc", 0), ("qc", 1), ("qc", 2), ("qc", 3), ("kpe", 0)]
        rope_tile = {"swq": SWQ, "swk": SWK, "gaq": GAQ, "gak": GAK, "qc": QC, "kpe": KPE}
        norm_jobs = [("ga_q", [GAQ], HD), ("ga_q", [GAQ + 1], HD), ("ga_k", [GAK], HD),
                     ("mla_q", [CQ, CQ + 1], 256), ("mla_kv", [CKV], 128)]

        def lo(l):
            return 0 if l < DEPTH - 1 else CTX

        def key_only(l, name):
            return 0 if name in ("swk", "gak", "kpe", "ga_k", "mla_kv") else lo(l)

        def acc_tokens(t):
            return Shifted(acc[:, t, :])

        def attention_products(l):
            q, a = slice(lo(l), TOK), slice(0, TOK)
            return [(SWQ, 0, P, q, "features"), (SWQ + 1, P, P, q, "features"),
                    (SWK, 0, P, a, "features"), (SWV, P, P, a, "tokens"),
                    (CQ, 0, P, q, "features"), (CQ + 1, P, P, q, "features"),
                    (CKV, 0, P, a, "features"), (KPE, P, 96, a, "features"),
                    (GAQ, 0, P, q, "features"), (GAQ + 1, P, P, q, "features"),
                    (GAK, 0, P, a, "features"), (GAV, P, P, a, "tokens")]

        router_w = sb("router_w", [P, KD, EXPERTS])
        logit, pick1, pick2 = sb("logit", [P, 2, 8]), sb("pick1", [P, 2, 8]), sb("pick2", [P, 2, 8])
        scan8, gate8, rank8 = sb("scan8", [P, 2, 8]), sb("gate8", [P, 2, 8]), sb("rank8", [P, 2, 8])
        top = sb("top", [P, 2, 2])
        topd = sb("topd", [P, 2])
        over = sb("over", [P, 3, 8])
        over_f = sb("over_f", [P, 4])
        over_i = sb("over_i", [P, 4], I32)
        ftm = T(0, 4).rearrange("p a b -> p (a b)").rearrange("p (t d) -> p t d", t=2)
        acc = T(4, 4).rearrange("p a b -> p (a b)").rearrange("p (k t) -> p k t", k=KD)

        def part(name, shape, at):
            return nc.alloc_sbuf_tensor_at(name, shape, F32R, offset=at)

        def tile_at(i):
            return arena_at + 4 * TOK * i
        wh = part("weights_high", [P, 4, UW // 2], tile_at(25))
        wl = part("weights_low", [P, 4, UW // 2], tile_at(33))
        xh = part("tokens_high", [P, KD, SLOTS], tile_at(8))
        xl = part("tokens_low", [P, KD, SLOTS], tile_at(10))
        gh = part("hidden_high", [P, FT, SLOTS], tile_at(14))
        gl = part("hidden_low", [P, FT, SLOTS], hT_at)
        gact = T(12).rearrange("p (a f) -> p a f", a=2)
        ghid = T(13).rearrange("p (a f) -> p a f", a=2)
        ys = T(21, 2).rearrange("p a b -> p (a b)")
        pm = T(23).rearrange("p (g t s) -> p g t s", g=2, t=2)
        ptg = T(24)[:, 0:LAT]
        e_products, e_scalars, e_vectors = sem("e_products"), sem("e_scalars"), sem("e_vectors")
        by_name.update({s.name: s for s in (e_products, e_scalars, e_vectors)})
        base = {unit_used.name: DENSE_UNITS}

        def per_pass(s):
            return MOE_UNITS if s is unit_used else book.known.get(("pass", s.name), 1)

        def in_pass(i, *step):
            name, value = book.known.get(step, ("e_products", 1))
            s = by_name[name]
            if s is unit_used:
                return s, i * MOE_UNITS + value
            return s, (i + 1) * per_pass(s) + value

        block = ctx.enter_context(nc.Block())

        @block.sync
        def _(sp):
            sp.dma_start(vec[:], vecs).then_inc(vec_loaded, 16)
            sp.dma_start(ring[:, 0, :], wstream[0]).then_inc(unit_loaded[0], 16)
            sp.dma_start(xT[:], xin).then_inc(x_loaded, 16)
            for u in range(1, RING):
                sp.dma_start(ring[:, u, :], wstream[u]).then_inc(unit_loaded[u], 16)
            whole = ALL_UNITS // RING
            with sp.Fori(1, whole) as i:
                for s in range(RING):
                    sp.wait_ge(unit_used, RING * i + (s - RING + 1))
                    sp.dma_start(ring[:, s, :], wstream[RING * i + s]).then_inc(unit_loaded[s], 16)
            for u in range(RING * whole, ALL_UNITS):
                sp.wait_ge(unit_used, u - RING + 1)
                sp.dma_start(ring[:, u % RING, :], wstream[u]).then_inc(unit_loaded[u % RING], 16)
            sp.wait_ge(*done("over"))
            again = sp.value_load(over_i[0:1, 0:1], min_val=0, max_val=3)
            with sp.If(again > 0):
                with sp.Fori(0, again) as j:
                    e = sp.value_load(over_i[0:1, bass.ds(j + 1, 1)], min_val=0, max_val=EXPERTS - 1)
                    first = sp.snap(e * MOE_UNITS + DENSE_UNITS)
                    for q in range(MOE_UNITS):
                        s = (ALL_UNITS + q) % RING
                        sp.wait_ge(unit_used, j * MOE_UNITS + (ALL_UNITS + q - RING + 1))
                        sp.dma_start(ring[:, s, :], wstream[first + q]).then_inc(unit_loaded[s], 16)
            sp.wait_ge(*done("final", KD - 1))
            sp.dma_start(out, hT[:, :, CTX:TOK]).then_inc(out_stored, 16)
            sp.wait_ge(out_stored, 16)

        @block.tensor
        def _(pe):
            unit = [0]

            def next_unit():
                u = unit[0]
                unit[0] += 1
                pe.wait_ge(unit_loaded[u % RING], 16 * (u // RING + 1))
                return ring[:, u % RING, :]

            def mm(o, lhsT, rhs, first=True, last=True):
                return nc.tensor.matmul(o, lhsT, rhs, start=first, stop=last)

            def project(o, w, c0, width, cols):
                for k in range(KD):
                    ins = mm(o, w[:, k * UC + c0:k * UC + c0 + width], hT[:, k, cols], k == 0, k == KD - 1)
                return ins

            def modulation(l):
                for m in range(MOD_UNITS + 1):
                    if m < MOD_UNITS:
                        w = next_unit()
                        if m >= 2:
                            pe.wait_ge(*done("mod row", l, m - 2))
                        for k in range(KD):
                            ins = mm(bank[m % 2][0:2, 0:UC], csil[:, k, :], w[:, k * UC:(k + 1) * UC],
                                     k == 0, k == KD - 1)
                        ins.then_inc(*tick(unit_used, "mod row product", l, m))
                    if m >= 1:
                        pe.wait_ge(*done("mod row", l, m - 1))
                        if m >= 3:
                            pe.wait_ge(*done("mod", l, m - 3))
                        for c in range(2):
                            ins = nc.tensor.transpose(bank[3 - m % 2][:, 2 * c:2 * c + 2],
                                                      T(ROWS)[0:2, ((m - 1) % 2 * 2 + c) * P:((m - 1) % 2 * 2 + c + 1) * P],
                                                      C("ident", 2)[0:2, :])
                        ins.then_inc(*tick(products, "mod product", l, m - 1))

            def mean_square(tag, cols):
                for k in range(KD):
                    pe.wait_ge(*done("square", tag, k))
                    ins = mm(bank[0][:, cols], C("ones"), T(NSQ + k)[:, cols], k == 0, k == KD - 1)
                ins.then_inc(*tick(products, "mean square", tag))

            def rwkv_in(l):
                pe.wait_ge(*done("h", l, 1, KD - 1))
                for t in range(8):
                    if t % 2 == 0:
                        w = next_unit()
                    if t >= 4:
                        pe.wait_ge(*done("f0", l, t - 4))
                    ins = project(bank[t % 4][:], w, t % 2 * P, P, slice(0, TOK))
                    ins.then_inc(*tick(products if t % 2 == 0 else unit_used, "f product", l, t))

            def low_rank(l):
                pe.wait_ge(small_loaded, 16 * (l + 1))
                pe.wait_ge(*done("shift", l, 7))
                for n, name in enumerate(("w1", "a1", "g1") + (("v1",) if l else ())):
                    wid = 32 if name == "v1" else P
                    for k in range(2):
                        ins = mm(bank[n][0:wid, :], S(name, k * wid, wid), T(Z_ + k), k == 0, k == 1)
                    ins.then_inc(*tick(products, "inner product", l, name))
                for j in range(2):
                    pe.wait_ge(*done("inner", l, "g1"))
                    mm(bank[4 + j][:], S("g2", j * P), T(GH_)).then_inc(*tick(products, "g product", l, j))
                for j in range(2):
                    if l:
                        pe.wait_ge(*done("inner", l, "v1"))
                        mm(bank[6 + j][:], S("v2", j * P)[0:32, :], T(VH_)[0:32, :])\
                            .then_inc(*tick(products, "v product", l, j))
                for j in range(2):
                    pe.wait_ge(*done("kk square", l, j))
                    mm(bank[j][:], C("heads"), T(TMP_ + j)).then_inc(*tick(products, "kk sum", l, j))
                pe.wait_ge(*done("v", l, 1))
                pe.wait_ge(*done("g", l, 1))
                for c in range(NCH):
                    if c % 2 == 0 and l:
                        pe.wait_ge(*done("v gate", l, 1))
                    for j in range(2):
                        ins = nc.tensor.transpose(bank[6 + c // 2][:, (c % 2 * 2 + j) * P:(c % 2 * 2 + j + 1) * P],
                                                  T(V_ + j)[:, c * CH:(c + 1) * CH], C("ident"))
                    if c % 2:
                        ins.then_inc(*tick(products, "v turned", l, c // 2))

            def direction(l, d):
                for j in range(2):
                    if j == 0 and d == 0:
                        pe.wait_ge(*done("kk root", l, 1))
                        pe.wait_ge(*done("inner", l, "a1"))
                    if d == 1:
                        pe.wait_ge(*done("group end", l, 3))
                    half_rows = slice(HD * d, HD * d + HD)
                    mm(bank[j][:], S("w2", j * P)[half_rows, :], T(TH_)[half_rows, :])\
                        .then_inc(*tick(products, "decay product", l, d, j))
                    if j == 0 and d == 0:
                        pe.wait_ge(*done("g", l, 1))
                        pe.wait_ge(*done("inner", l, "g1"))
                    mm(bank[2 + j][:], S("a2", j * P)[half_rows, :], T(AH_)[half_rows, :])\
                        .then_inc(*tick(products, "rate product", l, d, j))

            def solve_and_scan(l, n):
                d, c = groups[n]
                cols = slice(c * CH, (c + 1) * CH)

                def four(o, left, right, p, kind):
                    for q in range(2):
                        ins = mm(o[:, (2 * kind + q) * P:(2 * kind + q + 1) * P], left[:, q, :], right[:, q, :])
                    return ins
                for p in range(2):
                    if n % 4 == 0:
                        pe.wait_ge(*done("hats", l, d, 1))
                        pe.wait_ge(*done("rate read", l, d, 1))
                        if n == 0:
                            pe.wait_ge(*done("v tokens", l, 1))
                    else:
                        pe.wait_ge(*done("group end", l, n - 1))
                    for q in range(2):
                        a_r = ar[rows(p), q, c, :, :]
                        mm(bank[p][:, 2 * q * P:2 * q * P + 2 * P], T(BH_ + q)[rows(p), cols], a_r)
                    for q in range(2):
                        a_r = ar[rows(p), q, c, :, :]
                        mm(bank[2 + p][:, 2 * q * P:2 * q * P + 2 * P], T(KH_ + q)[rows(p), cols], a_r)
                    for q in range(2):
                        ins = mm(bank[4 + p][:, q * P:(q + 1) * P], ar[rows(p), q, c, 0, :], T(BH_ + q)[rows(p), cols])
                    ins.then_inc(*tick(products, "gram", l, n, p))
                for p in range(2):
                    pe.wait_ge(*done("masked D", l, n, p))
                    four(bank[6 + p], DD[:, p, 1], DD[:, p, 0], p, 0)
                    four(bank[6 + p], DD[:, p, 0], DD[:, p, 1], p, 1).then_inc(*tick(products, "D2 product", l, n, p))
                for p in range(2):
                    pe.wait_ge(*done("D2", l, n, p))
                    pe.wait_ge(*done("masked", l, n, p))
                    four(bank[p], D2[:, p, 1], D2[:, p, 0], p, 0)
                    four(bank[p], D2[:, p, 0], D2[:, p, 1], p, 1).then_inc(*tick(products, "D4 product", l, n, p))
                    pe.wait_ge(*done("F1", l, n, p))
                    four(bank[2 + p], D2[:, p, 0], FG[:, p, 0], p, 0).then_inc(*tick(products, "F2 product", l, n, p))
                for p in range(2):
                    pe.wait_ge(*done("D4", l, n, p))
                    four(bank[4 + p], DD[:, p, 1], DD[:, p, 0], p, 0).then_inc(*tick(products, "D8 product", l, n, p))
                    pe.wait_ge(*done("F2", l, n, p))
                    four(bank[6 + p], DD[:, p, 0], FG[:, p, 0], p, 0).then_inc(*tick(products, "F3 product", l, n, p))
                for p in range(2):
                    pe.wait_ge(*done("D8", l, n, p))
                    pe.wait_ge(*done("F3", l, n, p))
                    four(bank[p], D8[:, p], FG[:, p, 0], p, 0).then_inc(*tick(products, "F4 product", l, n, p))
                pe.wait_ge(*done("F3", l, n, 0))
                for i, src in enumerate((BH_, BH_ + 1, KH_, KH_ + 1)):
                    ins = nc.tensor.transpose(bank[6][:, i * P:(i + 1) * P], T(src)[:, cols], C("ident"))
                ins.then_inc(*tick(products, "bk turned", l, n))
                for p in range(2):
                    pe.wait_ge(*done("F4", l, n, p))
                    four(bank[2 + p], EA[:, p, 0], FG[:, p, 0], p, 0)
                    four(bank[2 + p], FG[:, p, 0], EA[:, p, 0], p, 1).then_inc(*tick(products, "Z product", l, n, p))
                for p in range(2):
                    pe.wait_ge(*done("Z", l, n, p))
                    four(bank[4 + p], DD[:, p, 1], DD[:, p, 0], p, 0)
                    four(bank[4 + p], DD[:, p, 0], DD[:, p, 1], p, 1).then_inc(*tick(products, "Z2 product", l, n, p))
                for p in range(2):
                    pe.wait_ge(*done("Z2", l, n, p))
                    if p == 0:
                        pe.wait_ge(*done("bk", l, n))
                    four(bank[6 + p], D2[:, p, 0], D2[:, p, 1], p, 0)\
                        .then_inc(*tick(products, "Z4 product", l, n, p))
                    pe.wait_ge(*done("G1", l, n, p))
                    four(bank[p], D2[:, p, 1], FG[:, p, 1], p, 0).then_inc(*tick(products, "G2 product", l, n, p))
                for p in range(2):
                    pe.wait_ge(*done("Z4", l, n, p))
                    pe.wait_ge(*done("G2", l, n, p))
                    four(bank[2 + p], D8[:, p], FG[:, p, 1], p, 0).then_inc(*tick(products, "G3 product", l, n, p))

                def vrows(p, q):
                    return vt[:, c, (2 * q + p) * HD:(2 * q + p + 1) * HD]
                for p in range(2):
                    pe.wait_ge(*done("state", l, n, p))
                    for q in range(2):
                        o = bank[4 + p][:, q * HD:(q + 1) * HD]
                        mm(o, ar[rows(p), q, c, 0, :], state[rows(p), q, :], True, False)
                        ins = mm(o, EA[:, p, 1, q, :], vrows(p, q), False, True)
                    ins.then_inc(*tick(products, "u0 product", l, n, p))
                for p in range(2):
                    pe.wait_ge(*done("u0", l, n, p))
                    for q in range(2):
                        ins = mm(bank[6 + p][:, q * HD:(q + 1) * HD], FG[:, p, 0, q, :], u0[:, p, q, :])
                    ins.then_inc(*tick(products, "u1 product", l, n, p))
                for p in range(2):
                    pe.wait_ge(*done("u1", l, n, p))
                    pe.wait_ge(*done("G3", l, n, p))
                    for q in range(2):
                        ins = mm(bank[p][:, q * HD:(q + 1) * HD], FG[:, p, 1, q, :], u1[:, p, q, :])
                    ins.then_inc(*tick(products, "u product", l, n, p))
                for p in range(2):
                    pe.wait_ge(*done("u", l, n, p))
                    for q in range(2):
                        o = bank[4 + p][rows(p), q * HD:(q + 1) * HD]
                        mm(o, bk[:, (2 * q + p) * HD:(2 * q + p + 1) * HD], uu[:, p, q, :], True, False)
                        ins = mm(o, bk[:, 2 * P + (2 * q + p) * HD:2 * P + (2 * q + p + 1) * HD], vrows(p, q), False, True)
                    ins.then_inc(*tick(products, "state product", l, n, p))
                    if c * CH >= lo(l):
                        for q in range(2):
                            o = bank[2 + p][rows(p), q * P:(q + 1) * P]
                            mm(o, state[rows(p), q, :], ar[rows(p), q, c, 1, :], True, False)
                            mm(o, uu[:, p, q, :], AR2[:, p, 0, q, :], False, False)
                            ins = mm(o, vrows(p, q), AR2[:, p, 1, q, :], False, True)
                        ins.then_inc(*tick(products, "y product", l, n, p))

            def head_norm(l):
                cols = slice(lo(l), TOK)
                for j in range(2):
                    pe.wait_ge(*done("group end", l, 7))
                    mm(bank[j][:, cols], C("heads"), T(Y_ + j)[:, cols]).then_inc(*tick(products, "y sum", l, j))
                for j in range(2):
                    pe.wait_ge(*done("y square", l, j))
                    mm(bank[2 + j][:, cols], C("heads"), T(TMP_ + j)[:, cols]).then_inc(*tick(products, "y var", l, j))
                for j in range(2):
                    pe.wait_ge(*done("bonus in", l, j))
                    mm(bank[4 + j][:, cols], C("heads"), T(LW_ + j)[:, cols]).then_inc(*tick(products, "bonus", l, j))

            def attention_in(l):
                outs = attention_products(l)
                for n, (dst, c0, width, cols, kind) in enumerate(outs):
                    if n % 2 == 0:
                        w = next_unit()
                    if n >= 4:
                        pe.wait_ge(*done("taken", l, n - 4))
                    elif n < 2:
                        pe.wait_ge(*done("y centred", l, 1))
                    else:
                        pe.wait_ge(*done("y root", l, 1))
                    if kind == "features":
                        ins = project(bank[n % 4][0:width, cols], w, c0, width, cols)
                    else:
                        for b in range(4):
                            for k in range(KD):
                                ins = mm(bank[n % 4][:, b * P:(b + 1) * P], hT[:, k, b * P:(b + 1) * P],
                                         w[:, k * UC + c0:k * UC + c0 + P], k == 0, k == KD - 1)
                    ins.then_inc(*tick(products if n % 2 == 0 else unit_used, "attention product", l, n))

            def attention_prep(l):
                pe.wait_ge(*done("taken", l, 11))
                for n, (name, tiles, width) in enumerate(norm_jobs):
                    cols = slice(key_only(l, name), TOK)
                    for i in range(len(tiles)):
                        pe.wait_ge(*done("prep square", l, n, i))
                        ins = mm(bank[4 + n % 4][:, cols], C("heads" if width == HD else "ones"),
                                 T(SCR + n % 4 * 2 + i)[:, cols], i == 0, i == len(tiles) - 1)
                    ins.then_inc(*tick(products, "prep sum", l, n))
                cols = slice(lo(l), TOK)
                for h in range(4):
                    pe.wait_ge(*done("prep normed", l, 3))
                    for k in range(2):
                        ins = mm(bank[h][0:96, cols], S("uq", k * 384 + h * 96, 96), T(CQ + k)[:, cols], k == 0, k == 1)
                    ins.then_inc(*tick(products, "q up", l, h))
                for h in range(4):
                    pe.wait_ge(*done("prep normed", l, 4))
                    if h < 4:
                        pe.wait_ge(*done("q taken", l, h))
                    mm(bank[h][0:HD, :], S("ukv", h * HD, HD), T(CKV)).then_inc(*tick(products, "k up", l, h))
                for i in range(2):
                    for b in range(2):
                        ins = mm(bank[4 + i][:, b * 256:(b + 1) * 256], T(CKV)[:, (2 * i + b) * P:(2 * i + b + 1) * P],
                                 S("ukv", 256, 256))
                    ins.then_inc(*tick(products, "v up", l, i))
                lat = slice(CTX, TOK)
                for n, (name, i) in enumerate(rope_jobs):
                    if name == "qc":
                        pe.wait_ge(*done("q taken", l, i))
                    if n >= 2:
                        pe.wait_ge(*done("roped", l, n - 2))
                    n96 = name in ("qc", "kpe")
                    r = slice(0, 96) if n96 else slice(0, P)
                    t = rope_tile[name] + i
                    mm(bank[6 + n % 2][r, 0:LAT], C("rot96" if n96 else "rot64")[r, r.start:r.stop], T(t)[r, lat])\
                        .then_inc(*tick(products, "rotated", l, n))

            def attention(l):
                units = heads_of(l)
                for n in range(len(units) + 3):
                    if n < len(units):
                        br, h, q, nk = units[n]
                        if n == 0:
                            pe.wait_ge(*done("roped", l, len(rope_jobs) - 1))
                            pe.wait_ge(*done("v taken", l, 1))
                            pe.wait_ge(*done("k taken", l, 3))
                            pe.wait_ge(*done("kpe spread", l, 3))
                        if n >= 3:
                            pe.wait_ge(*done("exp", l, n - 3))
                            pe.wait_ge(*done("max", l, n - 3))
                        if br == 1:
                            left, right = T(QC + h)[0:96, q:q + P], T(KC + h)[0:96, 0:nk]
                        else:
                            tq, tk = ((SWQ, SWK), None, (GAQ, GAK))[br]
                            half_rows = slice(HD * (h // 2), HD * (h // 2) + HD)
                            left, right = T(tq + h % 2)[half_rows, q:q + P], T(tk)[half_rows, 0:nk]
                        mm(bank[n % 3][:, 0:nk], left, right).then_inc(*tick(products, "scores", l, n))
                    if 2 <= n <= len(units) + 1:
                        m = n - 2
                        nk = units[m][3]
                        pe.wait_ge(*done("probs", l, m))
                        if m >= 2:
                            pe.wait_ge(*done("turned", l, m - 2))
                        for b in range(nk // P):
                            ins = nc.tensor.transpose(bank[3 + m % 2][:, b * P:(b + 1) * P],
                                                      T(PB + m % 3)[:, b * P:(b + 1) * P], C("ident"))
                        ins.then_inc(*tick(products, "turn", l, m))
                    if n >= 3:
                        m = n - 3
                        br, h, q, nk = units[m]
                        pe.wait_ge(*done("turned", l, m))
                        if m >= 2:
                            pe.wait_ge(*done("head out", l, m - 2))
                        for b in range(nk // P):
                            if br == 1:
                                v = T(VC, 2).rearrange("p a (b f) -> p (a b) f", f=256)[:, b, h * HD:(h + 1) * HD]
                            else:
                                v = T((SWV, None, GAV)[br])[:, b * P + h // 2 * HD:b * P + h // 2 * HD + HD]
                            ins = mm(bank[5 + m % 2][rows(h), 0:P], v, T(PTB + m % 2)[:, b * P:(b + 1) * P],
                                     b == 0, b == nk // P - 1)
                        ins.then_inc(*tick(products, "head", l, m))

            def merge(l):
                cols = slice(lo(l), TOK)
                last = len(heads_of(l)) - 1
                for cp in range(4):
                    for i in range(8):
                        if i % 2 == 0:
                            w = next_unit()
                        n = cp * 8 + i
                        if n >= 4:
                            pe.wait_ge(*done("gate", l, n - 4))
                        elif n == 0:
                            pe.wait_ge(*done("head out", l, last))
                        ins = project(bank[n % 4][:, cols], w, i % 2 * P, P, cols)
                        ins.then_inc(*tick(products if i % 2 == 0 else unit_used, "gate product", l, n))
                    w = next_unit()
                    for i in range(8):
                        n = cp * 8 + i
                        if n >= 4:
                            pe.wait_ge(*done("merged", l, n - 4))
                        for k in range(2):
                            r = (i // 2 * 2 + k) * UC + i % 2 * P
                            ins = mm(bank[4 + n % 4][:, cols], w[:, r:r + P], T(i // 2 * 2 + k)[:, cols], k == 0, k == 1)
                        ins.then_inc(*tick(products if i < 7 else unit_used, "branch product", l, n))
                for t in range(KD):
                    if t % 2 == 0:
                        w = next_unit()
                    pe.wait_ge(*done("merged", l, 31))
                    if t >= 4:
                        pe.wait_ge(*done("residual", l, 1, t - 4))
                    else:
                        pe.wait_ge(*done("gate", l, 31))
                    for k in range(KD):
                        ins = mm(bank[t % 4][:, cols], w[:, k * UC + t % 2 * P:k * UC + t % 2 * P + P],
                                 T(MT + k)[:, cols], k == 0, k == KD - 1)
                    ins.then_inc(*tick(products if t % 2 == 0 else unit_used, "out product", l, t))

            def dense_ffn(l):
                for p in range(PAIRS):
                    for half_ in range(2):
                        w = next_unit()
                        for c in range(2):
                            t = 2 * p + c
                            if t >= 4:
                                pe.wait_ge(*done("silu" if half_ == 0 else "hidden", l, t - 4))
                            elif t == 0 and half_ == 0:
                                pe.wait_ge(*done("h", l, 2, KD - 1))
                            ins = project(bank[4 * half_ + t % 4][:], w, c * P, P, slice(0, TOK))
                            ins.then_inc(*tick(products if c == 0 else unit_used, "w1" if half_ == 0 else "w3", l, t))
                for cp in range(4):
                    for kk in range(4):
                        w = next_unit()
                        if cp == 0 and kk == 0:
                            pe.wait_ge(*done("hidden", l, FT - 1))
                        if kk == 0 and cp >= 2:
                            pe.wait_ge(*done("residual", l, 2, 2 * cp - 3))
                        for c in range(2):
                            for k in range(7):
                                ins = mm(bank[cp % 2 * 2 + c][:], w[:, k * UC + c * P:k * UC + c * P + P],
                                         T(kk * 7 + k), kk == 0 and k == 0, kk == 3 and k == 6)
                            if kk == 3 and c == 0:
                                ins.then_inc(*tick(products, "down product", l, 2 * cp))
                        step = ("down product", l, 2 * cp + 1) if kk == 3 else ("down unit", l, cp, kk)
                        ins.then_inc(*tick(unit_used, *step))

            pe.wait_ge(*done("silu c"))
            pe.wait_ge(const_loaded, 16)
            modulation(0)
            for l in range(DEPTH):
                if l == 0:
                    pe.wait_ge(*done("mod", 0, MOD_UNITS - 1))
                mean_square(("n1", l), slice(0, TOK))
                rwkv_in(l)
                low_rank(l)
                direction(l, 0)
                for n in range(8):
                    if n == 4:
                        direction(l, 1)
                    solve_and_scan(l, n)
                head_norm(l)
                attention_in(l)
                attention_prep(l)
                attention(l)
                merge(l)
                pe.wait_ge(*done("residual", l, 1, KD - 1))
                mean_square(("n2", l), slice(lo(l), TOK))
                if l == 0:
                    dense_ffn(l)
                    pe.wait_ge(*done("residual", 0, 2, KD - 1))
                    modulation(1)
                    pe.wait_ge(*done("mod", 1, MOD_UNITS - 1))
            assert unit[0] == DENSE_UNITS, unit
            pe.wait_ge(router_loaded, 16)
            pe.wait_ge(*done("h", 1, 2, KD - 1))
            for t in range(2):
                for k in range(KD):
                    ins = mm(bank[1][:, 8 * t:8 * t + 8], hT[:, k, CTX + t * P:CTX + (t + 1) * P], router_w[:, k, :],
                             k == 0, k == KD - 1)
            ins.then_inc(*tick(products, "logits"))
            for i in range(4):
                for k in range(4):
                    ins = nc.tensor.transpose(bank[2 + i][:, k * P:(k + 1) * P],
                                              hT[:, i % 2 * 4 + k, CTX + i // 2 * P:CTX + (i // 2 + 1) * P], C("ident"))
                ins.then_inc(*tick(products, "tokens turned", i))
            pe.wait_ge(*done("picks"))
            mm(bank[6][:, 0:8], C("tri"), pick1[:, 0, :])
            mm(bank[6][:, 8:16], C("ones"), pick1[:, 0, :], True, False)
            mm(bank[6][:, 8:16], C("tri"), pick1[:, 1, :], False, True)
            mm(bank[6][:, 16:24], C("ones"), pick1[:, 0, :], True, False)
            mm(bank[6][:, 16:24], C("ones"), pick1[:, 1, :], False, True).then_inc(*tick(products, "ranks"))

            def expert_pass(i):
                def three(o, left, cols, v, first, last):
                    mm(o, left[0], wh[:, v % 4, cols], first, False)
                    mm(o, left[0], wl[:, v % 4, cols], False, False)
                    return mm(o, left[1], wh[:, v % 4, cols], False, last)
                pe.wait_ge(*in_pass(i, "tokens picked"))
                pe.wait_ge(*in_pass(i - 1, "added", 3))
                for b in range(2):
                    for k in range(4):
                        for t in range(2):
                            ins = mm(bank[b][:, k * P:(k + 1) * P], ftm[:, t, (4 * b + k) * P:(4 * b + k + 1) * P],
                                     pm[:, 0, t, :], t == 0, t == 1)
                    ins.then_inc(*tick(e_products, "gathered", b))
                for t in range(2):
                    ins = nc.tensor.transpose(bank[2][:, t * P:(t + 1) * P], pm[:, 1, t, :], C("ident"))
                ins.then_inc(*tick(e_products, "gates turned"))

                def turn_hidden(p):
                    pe.wait_ge(*in_pass(i, "hidden", p))
                    if p >= 2:
                        pe.wait_ge(*in_pass(i, "hidden low", p - 2))
                    elif p == 1:
                        pe.wait_ge(*in_pass(i, "gates kept"))
                    else:
                        pe.wait_ge(*in_pass(i - 1, "hidden low", PAIRS - 2))
                    for c in range(2):
                        ins = nc.tensor.transpose(bank[5 - 3 * (p % 2)][:, c * P:(c + 1) * P],
                                                  ghid[:, p % 2, c * P:(c + 1) * P], C("ident"))
                    ins.then_inc(*tick(e_products, "hidden turned", p))
                for p in range(PAIRS):
                    for n in range(2):
                        v = 4 * p + 2 * n
                        pe.wait_ge(*in_pass(i, "low", v))
                        if n == 0:
                            if p == 0:
                                pe.wait_ge(*in_pass(i, "gathered low", 1))
                            if p < 2:
                                pe.wait_ge(*in_pass(i - 1, "hidden", PAIRS - 2 + p))
                            else:
                                pe.wait_ge(*in_pass(i, "hidden", p - 2))
                        for k in range(KD):
                            if k == 4:
                                ins.then_inc(*tick(e_products, "half", v))
                                v += 1
                                pe.wait_ge(*in_pass(i, "low", v))
                            ins = three(bank[3 + p % 2][:, n * UC:(n + 1) * UC], (xh[:, k, :], xl[:, k, :]),
                                        slice(k % 4 * UC, (k % 4 + 1) * UC), v, k == 0, k == KD - 1)
                        ins.then_inc(*tick(e_products, "half", v))
                    if p:
                        turn_hidden(p - 1)
                turn_hidden(PAIRS - 1)
                for q in range(PAIRS):
                    if q == 0:
                        pe.wait_ge(*in_pass(i - 1, "y kept", 0))
                        pe.wait_ge(*in_pass(i - 1, "y kept", 1))
                    if q >= PAIRS - 1 or q == 0:
                        pe.wait_ge(*in_pass(i, "hidden low", PAIRS - 2 if q == 0 else PAIRS - 1))
                    for c in range(2):
                        v = 4 * PAIRS + 2 * q + c
                        pe.wait_ge(*in_pass(i, "low", v))
                        for n in range(2):
                            ins = three(bank[6 + n][:], (gh[:, 2 * q + c, :], gl[:, 2 * q + c, :]),
                                        slice(n * 512, n * 512 + 512), v,
                                        q == 0 and c == 0, q == PAIRS - 1 and c == 1)
                        ins.then_inc(*tick(e_products, "half", v))
                pe.wait_ge(*in_pass(i, "y kept", 0))
                pe.wait_ge(*in_pass(i, "y kept", 1))
                for g in range(4):
                    if g >= 2:
                        pe.wait_ge(*in_pass(i, "added", g - 2))
                    for c in range(2):
                        ins = mm(bank[g % 2][:, c * LAT:(c + 1) * LAT], ys[:, (2 * g + c) * P:(2 * g + c + 1) * P], ptg)
                    ins.then_inc(*tick(e_products, "scattered", g))
                book.known_next[("pass", e_products.name)] = book.reached(e_products)

            pe.sem_inc(e_products, per_pass(e_products))
            pe.wait_ge(*done("tokens kept", 3))
            with pe.Fori(0, EXPERTS) as i:
                expert_pass(i)
            pe.wait_ge(*done("over"))
            again = pe.value_load(over_i[0:1, 0:1], min_val=0, max_val=3)
            with pe.If(again > 0):
                with pe.Fori(0, again) as j:
                    book.again(e_products)
                    expert_pass(j + EXPERTS)
            mean_square(("final",), slice(CTX, TOK))

        @block.scalar
        def _(act):
            act.dma_start(cn[:], consts).then_inc(const_loaded, 16)
            act.dma_start(sm[:], small[0]).then_inc(small_loaded, 16)
            act.dma_start(router_w[:], router).then_inc(router_loaded, 16)

            def f(o, i, func, **kw):
                return nc.scalar.activation(o, i, func, **kw)

            def own():
                act.wait_ge(scalars, book.reached(scalars))

            def root(o, i, scale, eps, *step):
                f(o, i, ACT.Sqrt, scale=scale, bias=eps).then_inc(*tick(scalars, *step))

            def squares(tag, cols):
                for k in range(KD):
                    f(T(NSQ + k)[:, cols], xT[:, k, cols], ACT.Square).then_inc(*tick(scalars, "square", tag, k))
                act.wait_ge(*done("mean square", tag))
                root(T(NR)[:, cols], bank[0][:, cols], 1.0 / D, V("eps"), "root", tag)

            def modulate(l, which, cols_of):
                for k in range(KD):
                    act.wait_ge(*done("x scaled", (f"n{which}", l), k))
                    for n, (cols, s) in enumerate(cols_of):
                        ins = f(hT[:, k, cols], hT[:, k, cols], ACT.Identity, scale=gain[:, l, which - 1, k, s:s + 1],
                                bias=modT[:, l, (which - 1) * 24 + k, s:s + 1])
                    ins.then_inc(*tick(scalars, "h", l, which, k))

            act.wait_ge(vec_loaded, 16)
            f(csil[:], V("c", 0, 16).rearrange("p (s k) -> p k s", s=2), ACT.Silu).then_inc(*tick(scalars, "silu c"))
            act.wait_ge(x_loaded, 16)

            def modulation(l):
                for m in range(MOD_UNITS):
                    act.wait_ge(*done("mod row product", l, m))
                    if m >= 2:
                        act.wait_ge(*done("mod product", l, m - 2))
                    f(T(ROWS)[0:2, m % 2 * UC:(m % 2 + 1) * UC], bank[m % 2][0:2, 0:UC], ACT.Copy)\
                        .then_inc(*tick(scalars, "mod row", l, m))
            modulation(0)
            for l in range(DEPTH):
                both = [(slice(0, CTX), 1), (slice(CTX, TOK), 0)]
                if l == 1:
                    act.wait_ge(*done("residual", 0, 2, KD - 1))
                squares(("n1", l), slice(0, TOK))
                act.wait_ge(*done("gains", l))
                modulate(l, 1, both)
                act.wait_ge(*done("shift weights", l))
                for t in range(8):
                    act.wait_ge(*done("f product", l, t))
                    f(T(t), bank[t % 4][:], ACT.Copy).then_inc(*tick(scalars, "f", l, t))
                    f(T(R_ + t), bank[t % 4][:], ACT.Copy, scale=mu0[:, t:t + 1]).then_inc(*tick(scalars, "f0", l, t))
                for n, (name, func, dst) in enumerate((("w1", ACT.Tanh, TH_), ("a1", ACT.Copy, AH_),
                                                       ("g1", ACT.Sigmoid, GH_), ("v1", ACT.Copy, VH_))[:3 + l]):
                    act.wait_ge(*done("inner product", l, name))
                    wid = 32 if name == "v1" else P
                    f(T(dst)[0:wid, :], bank[n][0:wid, :], func).then_inc(*tick(scalars, "inner", l, name))
                for j in range(2):
                    act.wait_ge(*done("g product", l, j))
                    if j == 0:
                        act.wait_ge(*done("shift", l, 7))
                    f(T(G_ + j), bank[4 + j][:], ACT.Copy).then_inc(*tick(scalars, "g", l, j))
                if l:
                    for j in range(2):
                        act.wait_ge(*done("v product", l, j))
                        f(T(Q_ + j), bank[6 + j][:], ACT.Sigmoid, bias=V("v0", j)).then_inc(*tick(scalars, "v gate", l, j))
                for j in range(2):
                    act.wait_ge(*done("kk sum", l, j))
                    root(T(LW_ + j), bank[j][:], 1.0, V("eps_kk"), "kk root", l, j)
                for i in range(2):
                    act.wait_ge(*done("v turned", l, i))
                    f(T(VT_ + i), bank[6 + i][:], ACT.Copy).then_inc(*tick(scalars, "v tokens", l, i))

                def direction(d):
                    for j in range(2):
                        act.wait_ge(*done("decay product", l, d, j))
                        if d == 0:
                            act.wait_ge(*done("kk", l, 1))
                        else:
                            act.wait_ge(*done("group end", l, 3))
                        f(T(LW_ + j), bank[j][:], ACT.Sigmoid, bias=V("w0", l * 4 + d * 2 + j))\
                            .then_inc(*tick(scalars, "decay", l, d, j))
                        act.wait_ge(*done("rate product", l, d, j))
                        f(T(A_ + j), bank[2 + j][:], ACT.Sigmoid, bias=V("a0", l * 4 + d * 2 + j))\
                            .then_inc(*tick(scalars, "rate read", l, d, j))
                    for j in range(2):
                        act.wait_ge(*done("sums", l, d, j))
                        excl, incl, inv = (((LW_, 1.0), (Q_, 1.0), (Q_, -1.0)) if d == 0 else
                                           ((Q_, -1.0), (LW_, -1.0), (LW_, 1.0)))

                        def by_chunk(i):
                            return T(i).rearrange("p (c t) -> p c t", c=NCH)
                        f(ar[:, j, :, 0, :], by_chunk(excl[0] + j), ACT.Exp, scale=excl[1])
                        f(ar[:, j, :, 1, :], by_chunk(incl[0] + j), ACT.Exp, scale=incl[1])
                        f(T(TMP_ + j), T(inv[0] + j), ACT.Exp, scale=inv[1]).then_inc(*tick(scalars, "exps", l, d, j))
                    f(edec[:, :, :], half[:, :, :], ACT.Exp).then_inc(*tick(scalars, "chunk decay", l, d))

                def solve(n):
                    def copy(o, i, *step):
                        f(o, i, ACT.Copy).then_inc(*tick(scalars, *step, l, n, p))
                    for p in range(2):
                        act.wait_ge(*done("D2 product", l, n, p))
                        copy(T(M_ + 2 + p), bank[6 + p][:], "D2")
                    for p in range(2):
                        act.wait_ge(*done("D4 product", l, n, p))
                        act.wait_ge(*done("F1", l, n, p))
                        copy(T(M_ + p), bank[p][:], "D4")
                    for p in range(2):
                        act.wait_ge(*done("D8 product", l, n, p))
                        copy(D8[:, p], bank[4 + p][:, 0:256].rearrange("p (q t) -> p q t", q=2), "D8")
                    act.wait_ge(*done("bk turned", l, n))
                    if n % 4 == 0:
                        act.wait_ge(*done("hats", l, groups[n][0], 1))
                    f(bk, bank[6][:], ACT.Copy).then_inc(*tick(scalars, "bk", l, n))
                    for p in range(2):
                        act.wait_ge(*done("Z product", l, n, p))
                        copy(T(M_ + p), bank[2 + p][:], "Z")
                    for p in range(2):
                        act.wait_ge(*done("Z2 product", l, n, p))
                        copy(T(M_ + 2 + p), bank[4 + p][:], "Z2")
                    for p in range(2):
                        act.wait_ge(*done("Z4 product", l, n, p))
                        copy(D8[:, p], bank[6 + p][:, 0:256].rearrange("p (q t) -> p q t", q=2), "Z4")
                    for p in range(2):
                        act.wait_ge(*done("u1 product", l, n, p))
                        copy(u1[:, p], bank[6 + p][:, 0:P].rearrange("p (q v) -> p q v", q=2), "u1")
                direction(0)
                for n in range(8):
                    if n == 4:
                        direction(1)
                    solve(n)
                cols = slice(lo(l), TOK)
                for j in range(2):
                    act.wait_ge(*done("y centred", l, j))
                    f(T(TMP_ + j)[:, cols], T(Y_ + j)[:, cols], ACT.Square).then_inc(*tick(scalars, "y square", l, j))
                for j in range(2):
                    act.wait_ge(*done("y var", l, j))
                    root(T(Q_ + j)[:, cols], bank[2 + j][:, cols], 1.0 / HD, V("eps_gn"), "y root", l, j)
                for j in range(2):
                    act.wait_ge(*done("y scaled", l, j))
                    f(T(Y_ + j)[:, cols], T(Y_ + j)[:, cols], ACT.Identity, scale=V("ln_w", 2 * l + j),
                      bias=V("ln_b", 2 * l + j)).then_inc(*tick(scalars, "y affine", l, j))
                for n, (dst, c0, width, acols, kind) in enumerate(attention_products(l)):
                    act.wait_ge(*done("attention product", l, n))
                    if n == 0:
                        act.wait_ge(*done("branch a", l, 1))
                    f(T(dst)[0:width, acols], bank[n % 4][0:width, acols], ACT.Copy)\
                        .then_inc(*tick(scalars, "taken", l, n))
                own()
                for n, (name, tiles, width) in enumerate(norm_jobs):
                    ncols = slice(key_only(l, name), TOK)
                    if n == 4:
                        act.wait_ge(*done("prep normed", l, 0))
                    for i, t in enumerate(tiles):
                        f(T(SCR + n % 4 * 2 + i)[:, ncols], T(t)[:, ncols], ACT.Square)\
                            .then_inc(*tick(scalars, "prep square", l, n, i))
                    act.wait_ge(*done("prep sum", l, n))
                    root(T(SCR + n % 4 * 2)[:, ncols], bank[4 + n % 4][:, ncols], 1.0 / width, V("eps"),
                         "prep root", l, n)
                for h in range(4):
                    act.wait_ge(*done("q up", l, h))
                    f(T(QC + h)[0:96, cols], bank[h][0:96, cols], ACT.Copy).then_inc(*tick(scalars, "q taken", l, h))
                for h in range(4):
                    act.wait_ge(*done("k up", l, h))
                    f(T(KC + h)[0:HD, :], bank[h][0:HD, :], ACT.Copy).then_inc(*tick(scalars, "k taken", l, h))
                for i in range(2):
                    act.wait_ge(*done("v up", l, i))
                    f(T(VC + i), bank[4 + i][:], ACT.Copy).then_inc(*tick(scalars, "v taken", l, i))
                for h in range(4):
                    act.wait_ge(*done("roped", l, len(rope_jobs) - 1))
                    f(T(KC + h)[HD:96, :], T(KPE)[HD:96, :], ACT.Copy).then_inc(*tick(scalars, "kpe spread", l, h))
                units = heads_of(l)
                scale = [HD ** -0.5, 96 ** -0.5, HD ** -0.5]
                for n in range(len(units) + 2):
                    if n < len(units):
                        br, h, q, nk = units[n]
                        act.wait_ge(*done("max", l, n))
                        if n >= 3:
                            act.wait_ge(*done("turn", l, n - 3))
                            act.wait_ge(*done("probs", l, n - 3))
                        src = T(SB + n % 2)[:, 0:nk] if br == 0 and q >= CTX else bank[n % 3][:, 0:nk]
                        if br == 0:
                            f(es[:, n % 3:n % 3 + 1], V("sink", 4 * l + h), ACT.Exp, bias=nm[:, n % 3:n % 3 + 1])
                        f(T(PB + n % 3)[:, 0:nk], src, ACT.Exp, scale=scale[br], bias=nm[:, n % 3:n % 3 + 1],
                          accum_out=dn[:, n % 3:n % 3 + 1]).then_inc(*tick(scalars, "exp", l, n))
                    if n >= 2:
                        m = n - 2
                        nk = units[m][3]
                        act.wait_ge(*done("turn", l, m))
                        if m >= 2:
                            act.wait_ge(*done("head", l, m - 2))
                        f(T(PTB + m % 2)[:, 0:nk], bank[3 + m % 2][:, 0:nk], ACT.Copy)\
                            .then_inc(*tick(scalars, "turned", l, m))
                for n in range(32):
                    act.wait_ge(*done("gate product", l, n))
                    if n >= 8:
                        act.wait_ge(*done("merged", l, n - 8))
                    elif n == 0:
                        act.wait_ge(*done("head", l, len(units) - 1))
                    f(T(SG + n % 8)[:, cols], bank[n % 4][:, cols], ACT.Sigmoid).then_inc(*tick(scalars, "gate", l, n))
                act.wait_ge(*done("residual", l, 1, KD - 1))
                if l == 0:
                    act.dma_start(sm[:], small[1]).then_inc(small_loaded, 16)
                squares(("n2", l), cols)
                modulate(l, 2, both if l == 0 else both[1:])
                if l == 0:
                    for t in range(FT):
                        act.wait_ge(*done("w1", l, t))
                        if t >= 2:
                            act.wait_ge(*done("hidden", l, t - 2))
                        f(T(28 + t % 2), bank[t % 4][:], ACT.Silu).then_inc(*tick(scalars, "silu", l, t))
                    modulation(1)
            for i in range(4):
                act.wait_ge(*done("tokens turned", i))
                f(ftm[:, i // 2, i % 2 * 512:i % 2 * 512 + 512], bank[2 + i][:], ACT.Copy)\
                    .then_inc(*tick(scalars, "tokens kept", i))
            act.wait_ge(*done("top two"))
            f(topd[:], topd[:], ACT.Exp).then_inc(*tick(scalars, "top exp"))

            def expert_pass(i):
                def keep(o, src, after, *name):
                    act.wait_ge(*in_pass(i, *after))
                    f(o, src, ACT.Copy).then_inc(*tick(e_scalars, *name))

                def high(v):
                    at = DENSE_UNITS + v // 2
                    if v % 2 == 0:
                        act.wait_ge(unit_loaded[at % RING], i * (16 * MOE_UNITS // RING) + 16 * (at // RING + 1))
                    if v >= 4:
                        act.wait_ge(*in_pass(i, "half", v - 4))
                    else:
                        act.wait_ge(*in_pass(i - 1, "half", 2 * MOE_UNITS - 4 + v))
                    f(wh[:, v % 4, :], ring[:, at % RING, v % 2 * 1024:v % 2 * 1024 + 1024], ACT.Copy)\
                        .then_inc(*tick(e_scalars, "high", v))
                for v in range(4):
                    high(v)
                for b in range(2):
                    keep(xh[:, 4 * b:4 * b + 4, :], bank[b][:].rearrange("p (k t) -> p k t", k=4), ("gathered", b),
                         "gathered kept", b)
                keep(ptg, bank[2][:, 0:LAT], ("gates turned",), "gates kept")

                def keep_hidden(p):
                    keep(gh[:, 2 * p:2 * p + 2, :],
                         bank[5 - 3 * (p % 2)][:, 0:LAT].rearrange("p (k t) -> p k t", k=2), ("hidden turned", p),
                         "hidden kept", p)
                for p in range(PAIRS):
                    for v in (4, 5, 6):
                        high(4 * p + v)
                    act.wait_ge(*in_pass(i, "half", 4 * p + 3))
                    if p < 2:
                        act.wait_ge(*in_pass(i - 1, "hidden", PAIRS - 2 + p))
                    else:
                        act.wait_ge(*in_pass(i, "hidden", p - 2))
                    f(gact[:, p % 2, :], bank[3 + p % 2][:, 0:UC], ACT.Silu).then_inc(*tick(e_scalars, "silu", p))
                    high(4 * p + 7)
                    if p:
                        keep_hidden(p - 1)
                keep_hidden(PAIRS - 1)
                for v in range(4 * PAIRS + 4, 2 * MOE_UNITS):
                    high(v)
                keep(ys[:, 0:512], bank[6][:], ("half", 2 * MOE_UNITS - 1), "y kept", 0)
                book.known_next[("pass", e_scalars.name)] = book.reached(e_scalars)
            act.sem_inc(e_scalars, per_pass(e_scalars))
            with act.Fori(0, EXPERTS) as i:
                expert_pass(i)
            act.wait_ge(*done("over"))
            again = act.value_load(over_i[0:1, 0:1], min_val=0, max_val=3)
            with act.If(again > 0):
                with act.Fori(0, again) as j:
                    book.again(e_scalars)
                    expert_pass(j + EXPERTS)
            act.wait_ge(*done("residual", 1, 2, KD - 1))
            squares(("final",), slice(CTX, TOK))

        @block.vector
        def _(dve):
            vx = nc.vector

            def own():
                dve.wait_ge(vectors, book.reached(vectors))

            def step(ins, *name):
                ins.then_inc(*tick(vectors, *name))

            fresh = [0]

            def chain(ins):
                fresh[0] += 1
                ins.then_inc(*tick(vectors, "chain", fresh[0]))
                own()

            def modulation(l):
                for m in range(MOD_UNITS):
                    dve.wait_ge(*done("mod product", l, m))
                    o = modT[:, l, 2 * m:2 * m + 2, :]
                    b = V("b_mod", 48 * l + 2 * m, 2).unsqueeze(2).to_broadcast([P, 2, 2])
                    step(vx.tensor_tensor(o, bank[2 + m % 2][:, 0:4].rearrange("p (a b) -> p a b", a=2), b, ALU.add),
                         "mod", l, m)
                own()
                for which, name in ((0, "norm1"), (1, "norm2")):
                    sc = modT[:, l, 24 * which + 8:24 * which + 16, :]
                    g = V(name, KD * l, KD).unsqueeze(2).to_broadcast([P, KD, 2])
                    ins = vx.scalar_tensor_tensor(gain[:, l, which], sc, 1.0, g, ALU.add, ALU.mult)
                step(ins, "gains", l)

            def scale_x(tag, cols):
                dve.wait_ge(*done("root", tag))
                chain(vx.reciprocal(T(NR)[:, cols], T(NR)[:, cols]))
                for k in range(KD):
                    step(vx.tensor_tensor(hT[:, k, cols], xT[:, k, cols], T(NR)[:, cols], ALU.mult), "x scaled", tag, k)

            def shift(l):
                chain(vx.tensor_tensor(mu0[:], V("mu", 16 * l, 8), V("mu", 16 * l + 8, 8), ALU.add))
                chain(vx.tensor_scalar(mu0[:], mu0[:], -1.0, 1.0, ALU.mult, ALU.add))
                step(vx.tensor_scalar(omka[:], V("k_a", 2 * l, 2), -1.0, 1.0, ALU.mult, ALU.add), "shift weights", l)
                for t in range(8):
                    dve.wait_ge(*done("f0", l, t))
                    raw = T(t).rearrange("p (s n) -> p s n", s=2)
                    o = T(R_ + t).rearrange("p (s n) -> p s n", s=2)
                    chain(vx.scalar_tensor_tensor(o[:, :, 1:], raw[:, :, :-1], V("mu", 16 * l + t), o[:, :, 1:],
                                                  ALU.mult, ALU.add))
                    step(vx.scalar_tensor_tensor(o[:, :, :-1], raw[:, :, 1:], V("mu", 16 * l + 8 + t), o[:, :, :-1],
                                                 ALU.mult, ALU.add), "shift", l, t)

            def features(l):
                own()
                for j in range(2):
                    chain(vx.tensor_scalar(T(KK_ + j), T(K_ + j), V("k_k", 2 * l + j), None, ALU.mult))
                    dve.wait_ge(*done("inner", l, "a1"))
                    step(vx.tensor_tensor(T(TMP_ + j), T(KK_ + j), T(KK_ + j), ALU.mult), "kk square", l, j)
                for j in range(2):
                    if l == 0:
                        step(vx.tensor_copy(vfirst[:, j, :], T(V_ + j)), "v", l, j)
                    else:
                        dve.wait_ge(*done("v gate", l, j))
                        chain(vx.tensor_tensor(vfirst[:, j, :], vfirst[:, j, :], T(V_ + j), ALU.subtract))
                        chain(vx.tensor_tensor(vfirst[:, j, :], vfirst[:, j, :], T(Q_ + j), ALU.mult))
                        step(vx.tensor_tensor(T(V_ + j), T(V_ + j), vfirst[:, j, :], ALU.add), "v", l, j)
                for j in range(2):
                    dve.wait_ge(*done("kk root", l, j))
                    chain(vx.reciprocal(T(LW_ + j), T(LW_ + j)))
                    step(vx.tensor_tensor(T(KK_ + j), T(KK_ + j), T(LW_ + j), ALU.mult), "kk", l, j)

            def direction(l, d):
                for j in range(2):
                    dve.wait_ge(*done("decay", l, d, j))
                    chain(vx.tensor_scalar(T(LW_ + j), T(LW_ + j), -float(np.exp(-0.5)), None, ALU.mult))
                    for c in range(NCH):
                        cc = slice(c * CH, (c + 1) * CH)
                        ins = vx.tensor_tensor_scan(T(Q_ + j)[:, cc], C("ones"), T(LW_ + j)[:, cc], 0.0, ALU.mult, ALU.add)
                    chain(ins)
                    q = T(Q_ + j).rearrange("p (c t) -> p c t", c=NCH)
                    chain(vx.tensor_scalar(half[:, j, :], q[:, :, CH - 1], 0.5, None, ALU.mult))
                    chain(vx.tensor_tensor(q, q, half[:, j, :].unsqueeze(2).to_broadcast([P, NCH, CH]), ALU.subtract))
                    step(vx.tensor_tensor(T(LW_ + j), T(Q_ + j), T(LW_ + j), ALU.subtract), "sums", l, d, j)
                for j in range(2):
                    dve.wait_ge(*done("rate read", l, d, j))
                    chain(vx.tensor_scalar(T(KDIR_ + j), T(A_ + j), V("k_a", 2 * l + j), omka[:, j:j + 1], ALU.mult, ALU.add))
                    chain(vx.tensor_tensor(T(KDIR_ + j), T(KDIR_ + j), T(K_ + j), ALU.mult))
                    if d == 0:
                        chain(vx.tensor_copy(T(KS_ + j), T(KDIR_ + j)))
                    else:
                        chain(vx.tensor_tensor(T(KS_ + j), T(KS_ + j), T(KDIR_ + j), ALU.add))
                    chain(vx.tensor_tensor(T(A_ + j), T(A_ + j), T(KK_ + j), ALU.mult))
                    dve.wait_ge(*done("exps", l, d, j))

                    def by_chunk(i):
                        return T(i).rearrange("p (c t) -> p c t", c=NCH)
                    vx.scalar_tensor_tensor(ar[:, j, :, 0, :], ar[:, j, :, 0, :], -1.0, by_chunk(KK_ + j),
                                            ALU.mult, ALU.mult)
                    vx.tensor_tensor(ar[:, j, :, 1, :], ar[:, j, :, 1, :], by_chunk(R_ + j), ALU.mult)
                    vx.tensor_tensor(T(BH_ + j), T(A_ + j), T(TMP_ + j), ALU.mult)
                    step(vx.tensor_tensor(T(KH_ + j), T(KDIR_ + j), T(TMP_ + j), ALU.mult), "hats", l, d, j)
                for p in range(2):
                    step(vx.memset(state[rows(p), :, :], 0.0), "state", l, 4 * d, p)

            def solve(l, n):
                d, c = groups[n]
                up, low = ("0", "1") if d == 0 else ("1", "0")

                def mask(name):
                    return C(name).unsqueeze(1).to_broadcast([P, 2, P])

                def ident():
                    return mask("ident")
                if n % 4 == 0:
                    dve.wait_ge(*done("chunk decay", l, d))
                for p in range(2):
                    dve.wait_ge(*done("gram", l, n, p))
                    x1 = bank[p][:].rearrange("p (q s t) -> p q s t", q=2, s=2)
                    x2 = bank[2 + p][:].rearrange("p (q s t) -> p q s t", q=2, s=2)
                    x3 = bank[4 + p][:, 0:256].rearrange("p (q t) -> p q t", q=2)
                    vx.tensor_tensor(DD[:, p, 0], x3, mask("near" + low), ALU.mult)
                    step(vx.tensor_tensor(DD[:, p, 1], x1[:, :, 0, :], mask("near" + up), ALU.mult), "masked D", l, n, p)
                    vx.tensor_tensor(EA[:, p, 0], x3, mask("far" + low), ALU.mult)
                    vx.tensor_tensor(AR2[:, p, 0], x1[:, :, 1, :], mask("incl" + up), ALU.mult)
                    vx.tensor_tensor(EA[:, p, 1], x2[:, :, 0, :], mask("strict" + up), ALU.mult)
                    step(vx.tensor_tensor(AR2[:, p, 1], x2[:, :, 1, :], mask("incl" + up), ALU.mult), "masked", l, n, p)
                    dve.wait_ge(*done("masked D", l, n, p))
                    step(vx.tensor_tensor(FG[:, p, 0], DD[:, p, 1], ident(), ALU.add), "F1", l, n, p)

                def add(kind, b, name, p):
                    dve.wait_ge(*done(name + " product", l, n, p))
                    src = bank[b][:, 0:256].rearrange("p (q t) -> p q t", q=2)
                    step(vx.tensor_tensor(FG[:, p, kind], FG[:, p, kind], src, ALU.add), name, l, n, p)
                own()
                for name, b in (("F2", 2), ("F3", 6), ("F4", 0)):
                    for p in range(2):
                        add(0, b + p, name, p)
                    own()
                for p in range(2):
                    dve.wait_ge(*done("Z", l, n, p))
                    step(vx.tensor_tensor(FG[:, p, 1], DD[:, p, 0], ident(), ALU.add), "G1", l, n, p)
                own()
                for name, b in (("G2", 0), ("G3", 2)):
                    for p in range(2):
                        add(1, b + p, name, p)
                    own()
                for p in range(2):
                    dve.wait_ge(*done("u0 product", l, n, p))
                    step(vx.tensor_copy(u0[:, p], bank[4 + p][:, 0:P].rearrange("p (q v) -> p q v", q=2)), "u0", l, n, p)
                for p in range(2):
                    dve.wait_ge(*done("u product", l, n, p))
                    step(vx.tensor_copy(uu[:, p], bank[p][:, 0:P].rearrange("p (q v) -> p q v", q=2)), "u", l, n, p)
                last = n % 4 == 3
                if not last:
                    nxt = groups[n + 1][1]
                    chain(vx.tensor_tensor(scl[:], edec[:, :, c], edec[:, :, nxt], ALU.mult))
                for p in range(2):
                    r = rows(p)
                    dve.wait_ge(*done("state product", l, n, p))
                    has_y = c * CH >= lo(l)
                    if has_y:
                        dve.wait_ge(*done("y product", l, n, p))
                        y = T(Y_, 2)[r, :, c * CH:(c + 1) * CH]
                        src = bank[2 + p][r, 0:256].rearrange("p (q t) -> p q t", q=2)
                        if d == 0:
                            ins = vx.tensor_copy(y, src)
                        else:
                            ins = vx.tensor_tensor(y, y, src, ALU.add)
                        if last:
                            chain(ins)
                    if not last:
                        src = bank[4 + p][r, 0:P].rearrange("p (q v) -> p q v", q=2)
                        chain(vx.tensor_tensor(state[r, :, :], state[r, :, :], src, ALU.add))
                        step(vx.tensor_tensor(state[r, :, :], state[r, :, :],
                                              scl[r, :].unsqueeze(2).to_broadcast([HD, 2, HD]), ALU.mult),
                             "state", l, n + 1, p)
                step(vx.memset(mx[:, 3:4], 0.0), "group end", l, n)

            def head_norm(l):
                cols = slice(lo(l), TOK)
                own()
                for j in range(2):
                    dve.wait_ge(*done("y sum", l, j))
                    step(vx.scalar_tensor_tensor(T(Y_ + j)[:, cols], bank[j][:, cols], -1.0 / HD, T(Y_ + j)[:, cols],
                                                 ALU.mult, ALU.add), "y centred", l, j)
                for j in range(2):
                    step(vx.scalar_tensor_tensor(T(LW_ + j)[:, cols], T(KS_ + j)[:, cols], V("r_k", 2 * l + j),
                                                 T(R_ + j)[:, cols], ALU.mult, ALU.mult), "bonus in", l, j)
                for j in range(2):
                    dve.wait_ge(*done("y root", l, j))
                    chain(vx.reciprocal(T(Q_ + j)[:, cols], T(Q_ + j)[:, cols]))
                    step(vx.tensor_tensor(T(Y_ + j)[:, cols], T(Y_ + j)[:, cols], T(Q_ + j)[:, cols], ALU.mult),
                         "y scaled", l, j)
                for j in range(2):
                    dve.wait_ge(*done("bonus", l, j))
                    dve.wait_ge(*done("y affine", l, j))
                    chain(vx.tensor_tensor(T(A_ + j)[:, cols], bank[4 + j][:, cols], T(V_ + j)[:, cols], ALU.mult))
                    chain(vx.tensor_tensor(T(A_ + j)[:, cols], T(A_ + j)[:, cols], T(Y_ + j)[:, cols], ALU.add))
                    step(vx.tensor_tensor(T(j)[:, cols], T(A_ + j)[:, cols], T(G_ + j)[:, cols], ALU.mult),
                         "branch a", l, j)

            def attention_prep(l):
                for n, (name, tiles, width) in enumerate(norm_jobs):
                    cols = slice(key_only(l, name), TOK)
                    dve.wait_ge(*done("prep root", l, n))
                    r = T(SCR + n % 4 * 2)[:, cols]
                    chain(vx.reciprocal(r, r))
                    for i, t in enumerate(tiles):
                        g = V(name, l * len(tiles) + i)
                        ins = vx.scalar_tensor_tensor(T(t)[:, cols], T(t)[:, cols], g, r, ALU.mult, ALU.mult)
                    step(ins, "prep normed", l, n)
                own()
                lat = slice(CTX, TOK)
                for n, (name, i) in enumerate(rope_jobs):
                    n96 = name in ("qc", "kpe")
                    r = slice(0, 96) if n96 else slice(0, P)
                    w = "96" if n96 else "64"
                    t = T(rope_tile[name] + i)[r, lat]
                    tmp = T(SCR + n % 8)[r, 0:LAT]
                    dve.wait_ge(*done("rotated", l, n))
                    vx.tensor_tensor(tmp, bank[6 + n % 2][r, 0:LAT], C("sin" + w, LAT)[r, :], ALU.mult)
                    chain(vx.tensor_tensor(t, t, C("cos" + w, LAT)[r, :], ALU.mult))
                    step(vx.tensor_tensor(t, t, tmp, ALU.add), "roped", l, n)

            def attention(l):
                units = heads_of(l)
                scale = [HD ** -0.5, 96 ** -0.5, HD ** -0.5]
                for n in range(len(units) + 4):
                    if n < len(units):
                        br, h, q, nk = units[n]
                        s, c1 = bank[n % 3], slice(n % 3, n % 3 + 1)
                        dve.wait_ge(*done("scores", l, n))
                        if n >= 3:
                            dve.wait_ge(*done("exp", l, n - 3))
                        if br == 0 and q >= CTX:
                            if n >= 2:
                                dve.wait_ge(*done("exp", l, n - 2))
                            m = T(SB + n % 2)
                            vx.tensor_copy(m[:, 0:CTX], s[:, 0:CTX])
                            chain(vx.tensor_tensor(m[:, CTX:TOK], s[:, CTX:TOK], C("band", LAT, (q - CTX) // P * LAT),
                                                   ALU.add))
                            src = m[:, 0:nk]
                        else:
                            src = s[:, 0:nk]
                        chain(vx.reduce_max(mx[:, c1], src, AX.X))
                        if br == 0:
                            chain(vx.tensor_scalar(mx[:, c1], mx[:, c1], scale[br], V("sink", 4 * l + h), ALU.mult, ALU.max))
                            step(vx.tensor_scalar(nm[:, c1], mx[:, c1], -1.0, None, ALU.mult), "max", l, n)
                        else:
                            step(vx.tensor_scalar(nm[:, c1], mx[:, c1], -scale[br], None, ALU.mult), "max", l, n)
                    if 1 <= n <= len(units):
                        m = n - 1
                        br, h, q, nk = units[m]
                        c1 = slice(m % 3, m % 3 + 1)
                        dve.wait_ge(*done("exp", l, m))
                        if br == 0:
                            chain(vx.tensor_tensor(dn[:, c1], dn[:, c1], es[:, c1], ALU.add))
                        chain(vx.reciprocal(rs[:, c1], dn[:, c1]))
                        pr = T(PB + m % 3)[:, 0:nk]
                        step(vx.tensor_scalar(pr, pr, rs[:, c1], None, ALU.mult), "probs", l, m)
                    if n >= 4:
                        m = n - 4
                        br, h, q, nk = units[m]
                        dve.wait_ge(*done("head", l, m))
                        step(vx.tensor_copy(T(2 * (br + 1) + h // 2)[rows(h), q:q + P], bank[5 + m % 2][rows(h), 0:P]),
                             "head out", l, m)

            def residual(l, which, t, src):
                g0 = (2, 5)[which - 1] * 8 + t
                segs = [(slice(0, CTX), 1), (slice(CTX, TOK), 0)][(0 if lo(l) == 0 else 1):]
                for cols, s in segs:
                    ins = vx.scalar_tensor_tensor(xT[:, t, cols], src[:, cols], modT[:, l, g0, s:s + 1], xT[:, t, cols],
                                                  ALU.mult, ALU.add)
                step(ins, "residual", l, which, t)

            def merge(l):
                cols = slice(lo(l), TOK)
                for n in range(32):
                    cp, i, c = n // 8, n % 8 // 2, n % 2
                    dve.wait_ge(*done("branch product", l, n))
                    dve.wait_ge(*done("gate", l, n))
                    m = T(MT + 2 * cp + c)[:, cols]
                    if i == 0:
                        step(vx.tensor_tensor(m, T(SG + n % 8)[:, cols], bank[4 + n % 4][:, cols], ALU.mult),
                             "merged", l, n)
                    else:
                        chain(vx.tensor_tensor(T(MTMP)[:, cols], T(SG + n % 8)[:, cols], bank[4 + n % 4][:, cols],
                                               ALU.mult))
                        step(vx.tensor_tensor(m, m, T(MTMP)[:, cols], ALU.add), "merged", l, n)
                        own()
                for t in range(KD):
                    dve.wait_ge(*done("out product", l, t))
                    residual(l, 1, t, bank[t % 4])

            modulation(0)
            for l in range(DEPTH):
                scale_x(("n1", l), slice(0, TOK))
                shift(l)
                features(l)
                direction(l, 0)
                for n in range(8):
                    if n == 4:
                        direction(l, 1)
                    solve(l, n)
                head_norm(l)
                attention_prep(l)
                attention(l)
                merge(l)
                scale_x(("n2", l), slice(lo(l), TOK))
                if l == 0:
                    for t in range(FT):
                        dve.wait_ge(*done("silu", l, t))
                        dve.wait_ge(*done("w3", l, t))
                        step(vx.tensor_tensor(T(t), T(28 + t % 2), bank[4 + t % 4][:], ALU.mult), "hidden", l, t)
                    for t in range(KD):
                        dve.wait_ge(*done("down product", l, t))
                        residual(l, 2, t, bank[t // 2 % 2 * 2 + t % 2])
                    modulation(1)
            dve.wait_ge(*done("logits"))
            chain(vx.tensor_copy(logit[:], bank[1][:, 0:16].rearrange("p (t e) -> p t e", t=2)))
            for n, pick in enumerate((pick1, pick2)):
                chain(vx.reduce_max(top[:, n, :], logit[:], AX.X))
                chain(vx.tensor_tensor(pick[:], logit[:], top[:, n, :].unsqueeze(2).to_broadcast([P, 2, 8]), ALU.is_equal))
                for t in range(2):
                    ins = vx.tensor_tensor_scan(scan8[:, t, :], C("ones", 8), pick[:, t, :], 0.0, ALU.mult, ALU.add)
                chain(ins)
                chain(vx.scalar_tensor_tensor(pick[:], scan8[:], 1.5, pick[:], ALU.is_lt, ALU.mult))
                if n == 0:
                    chain(vx.scalar_tensor_tensor(logit[:], pick[:], NEG, logit[:], ALU.mult, ALU.add))
            step(vx.tensor_tensor(topd[:], top[:, 1, :], top[:, 0, :], ALU.subtract), "top two")
            dve.wait_ge(*done("top exp"))
            chain(vx.tensor_scalar(top[:, 0, :], topd[:], 1.0, None, ALU.add))
            chain(vx.reciprocal(top[:, 0, :], top[:, 0, :]))
            chain(vx.tensor_tensor(top[:, 1, :], topd[:], top[:, 0, :], ALU.mult))
            chain(vx.tensor_tensor(gate8[:], pick1[:], top[:, 0, :].unsqueeze(2).to_broadcast([P, 2, 8]), ALU.mult))
            chain(vx.tensor_tensor(scan8[:], pick2[:], top[:, 1, :].unsqueeze(2).to_broadcast([P, 2, 8]), ALU.mult))
            chain(vx.tensor_tensor(gate8[:], gate8[:], scan8[:], ALU.add))
            step(vx.tensor_tensor(pick1[:], pick1[:], pick2[:], ALU.add), "picks")
            own()
            dve.wait_ge(*done("ranks"))
            chain(vx.tensor_tensor(rank8[:], bank[6][:, 0:16].rearrange("p (t e) -> p t e", t=2), pick1[:], ALU.mult))
            chain(vx.tensor_scalar(rank8[:], rank8[:], 1.0, None, ALU.subtract))
            chain(vx.tensor_scalar(over[:, 0, :], bank[6][:, 16:24], SLOTS + 0.5, None, ALU.is_gt))
            chain(vx.tensor_tensor_scan(over[:, 1, :], C("ones", 8), over[:, 0, :], 0.0, ALU.mult, ALU.add))
            chain(vx.tensor_copy(over_f[:, 0:1], over[:, 1, 7:8]))
            for j in range(3):
                chain(vx.scalar_tensor_tensor(over[:, 2, :], over[:, 1, :], float(j + 1), over[:, 0, :],
                                              ALU.is_equal, ALU.mult))
                chain(vx.tensor_tensor(over[:, 2, :], over[:, 2, :], C("lane8", 8), ALU.mult))
                chain(vx.reduce_sum(over_f[:, j + 1:j + 2], over[:, 2, :], AX.X))
            step(vx.tensor_copy(over_i[:], over_f[:]), "over")
            chain(vx.memset(acc[:], 0.0))

            def expert_pass(i, e, first_slot):
                iota = C("iota", SLOTS, first_slot)
                for t in range(2):
                    if t == 0:
                        dve.wait_ge(*in_pass(i - 1, "gates turned"))
                    vx.tensor_scalar(pm[:, 0, t, :], iota, rank8[:, t, bass.ds(e, 1)], None, ALU.is_equal)
                    ins = vx.tensor_scalar(pm[:, 1, t, :], iota, rank8[:, t, bass.ds(e, 1)],
                                           gate8[:, t, bass.ds(e, 1)], ALU.is_equal, ALU.mult)
                ins.then_inc(*tick(e_vectors, "tokens picked"))
                book.count[unit_used.name] = DENSE_UNITS

                def low(v):
                    at = (DENSE_UNITS + v // 2) % RING
                    dve.wait_ge(*in_pass(i, "high", v))
                    vx.tensor_tensor(wl[:, v % 4, :], ring[:, at, v % 2 * 1024:v % 2 * 1024 + 1024],
                                     wh[:, v % 4, :].bitcast(F32), ALU.subtract)\
                        .then_inc(*tick(unit_used if v % 2 else e_vectors, "low", v))
                for v in range(4):
                    low(v)
                for b in range(2):
                    dve.wait_ge(*in_pass(i, "gathered kept", b))
                    vx.tensor_tensor(xl[:, 4 * b:4 * b + 4, :], bank[b][:].rearrange("p (k t) -> p k t", k=4),
                                     xh[:, 4 * b:4 * b + 4, :].bitcast(F32), ALU.subtract)\
                        .then_inc(*tick(e_vectors, "gathered low", b))

                def hidden_low(p):
                    dve.wait_ge(*in_pass(i, "hidden kept", p))
                    vx.tensor_tensor(gl[:, 2 * p:2 * p + 2, :],
                                     bank[5 - 3 * (p % 2)][:, 0:LAT].rearrange("p (k t) -> p k t", k=2),
                                     gh[:, 2 * p:2 * p + 2, :].bitcast(F32), ALU.subtract)\
                        .then_inc(*tick(e_vectors, "hidden low", p))
                for p in range(PAIRS):
                    for v in (4, 5, 6):
                        low(4 * p + v)
                    dve.wait_ge(*in_pass(i, "silu", p))
                    if p >= 2:
                        dve.wait_ge(*in_pass(i, "hidden turned", p - 2))
                    vx.tensor_tensor(ghid[:, p % 2, :], gact[:, p % 2, :], bank[3 + p % 2][:, UC:2 * UC], ALU.mult)\
                        .then_inc(*tick(e_vectors, "hidden", p))
                    low(4 * p + 7)
                    if p:
                        hidden_low(p - 1)
                hidden_low(PAIRS - 1)
                for v in range(4 * PAIRS + 4, 2 * MOE_UNITS):
                    low(v)
                dve.wait_ge(*in_pass(i, "half", 2 * MOE_UNITS - 1))
                vx.tensor_copy(ys[:, 512:1024], bank[7][:]).then_inc(*tick(e_vectors, "y kept", 1))
                for g in range(4):
                    dve.wait_ge(*in_pass(i, "scattered", g))
                    part = acc[:, 2 * g:2 * g + 2, :]
                    vx.tensor_tensor(part, part, bank[g % 2][:].rearrange("p (c t) -> p c t", c=2), ALU.add)\
                        .then_inc(*tick(e_vectors, "added", g))
                dve.wait_ge(*in_pass(i, "added", 3))
                vx.memset(mx[:, 3:4], 0.0)
                book.known_next[("pass", e_vectors.name)] = book.reached(e_vectors)
            dve.sem_inc(e_vectors, per_pass(e_vectors))
            with dve.Fori(0, EXPERTS) as i:
                expert_pass(i, i, 0)
            again = dve.value_load(over_i[0:1, 0:1], min_val=0, max_val=3)
            with dve.If(again > 0):
                with dve.Fori(0, again) as j:
                    book.again(e_vectors)
                    e = dve.value_load(over_i[0:1, bass.ds(j + 1, 1)], min_val=0, max_val=EXPERTS - 1)
                    expert_pass(j + EXPERTS, e, SLOTS)
            own()
            for t in range(KD):
                residual(1, 2, t, acc_tokens(t))
            scale_x(("final",), slice(CTX, TOK))
            own()
            for k in range(KD):
                step(vx.tensor_scalar(hT[:, k, CTX:TOK], hT[:, k, CTX:TOK], V("final", k), None, ALU.mult), "final", k)

    return {**book.marks, **book.known_next}


def layouts(x, ctx, c, c_ctx, w_mod, b_mod, norm1, norm2, w_in, w_branch, w_out, rw_mu, rw_w0, rw_w1, rw_w2,
            rw_a0, rw_a1, rw_a2, rw_v0, rw_v1, rw_v2, rw_g1, rw_g2, rw_k_k, rw_k_a, rw_r_k, rw_ln_w, rw_ln_b,
            sw_sink, mla_q_norm, mla_w_uq, mla_kv_norm, mla_w_ukv, ga_q_norm, ga_k_norm, ffn_w1, ffn_w3, ffn_w2,
            moe_router, moe_w1, moe_w3, moe_w2, final_norm):
    stream = np.zeros((ALL_UNITS, P, UW), np.float32)
    n = 0

    def put(tiles):
        nonlocal n
        k, _, w = tiles.shape
        stream[n].reshape(P, KD, UC)[:, :k, :w] = tiles.transpose(1, 0, 2)
        n += 1

    def by_columns(m, c0=0, c1=None):
        t = m.reshape(-1, P, m.shape[1])
        for a in range(c0, m.shape[1] if c1 is None else c1, UC):
            put(t[:, :, a:a + UC])

    def swap_heads(cols):
        return np.concatenate([np.arange(HD) + cols + HD * h for h in (0, 2, 1, 3)])

    def mixer(l):
        w = w_in[l]
        t = w.reshape(KD, P, -1)
        by_columns(w, 0, 1024)
        put(t[:, :, swap_heads(1024)])
        put(t[:, :, 1280:1536])
        put(t[:, :, 1536:1792])
        put(np.concatenate([t[:, :, 1792:1920], np.zeros((KD, P, HD), np.float32), t[:, :, 1920:1952]], 2))
        put(t[:, :, swap_heads(1952)])
        put(t[:, :, 2208:2464])
        gates = t[:, :, 2464:]
        wb = w_branch[l].reshape(KD, P, D)
        for cp in range(4):
            for i in range(4):
                put(gates[:, :, i * D + cp * UC:i * D + (cp + 1) * UC])
            put(wb[:, :, cp * UC:(cp + 1) * UC])
        by_columns(w_out[l])

    by_columns(w_mod[0])
    mixer(0)
    for a in range(0, FF, UC):
        put(ffn_w1[0].reshape(KD, P, FF)[:, :, a:a + UC])
        put(ffn_w3[0].reshape(KD, P, FF)[:, :, a:a + UC])
    for cp in range(4):
        for kk in range(4):
            put(ffn_w2[0].reshape(FT, P, D)[7 * kk:7 * kk + 7, :, cp * UC:(cp + 1) * UC])
    by_columns(w_mod[1])
    mixer(1)
    assert n == DENSE_UNITS
    e = stream[n:].reshape(EXPERTS, MOE_UNITS, P, UW)
    for i in range(EXPERTS):
        wide = e[i, :2 * PAIRS].reshape(PAIRS, 2, P, KD, UC)
        wide[:, 0] = moe_w1[0, i].reshape(KD, P, PAIRS, UC).transpose(2, 1, 0, 3)
        wide[:, 1] = moe_w3[0, i].reshape(KD, P, PAIRS, UC).transpose(2, 1, 0, 3)
        e[i, 2 * PAIRS:].reshape(PAIRS, P, 2, D)[:] = moe_w2[0, i].reshape(PAIRS, 2, P, D).transpose(0, 2, 1, 3)

    small = np.zeros((DEPTH, P, NSM), np.float32)
    for l in range(DEPTH):
        def fill(name, m):
            small[l, :m.shape[0], SM[name]:SM[name] + m.shape[1]] = m

        def two(m):
            return m.reshape(2, P, -1).transpose(1, 0, 2).reshape(P, -1)
        fill("w1", two(np.concatenate([rw_w1[l, 0], rw_w1[l, 1]], 1)))
        fill("a1", two(np.concatenate([rw_a1[l, 0], rw_a1[l, 1]], 1)))
        fill("g1", two(rw_g1[l]))
        fill("w2", rw_w2[l].reshape(P, 256))
        fill("a2", rw_a2[l].reshape(P, 256))
        fill("g2", rw_g2[l])
        if l:
            fill("v1", two(rw_v1[l - 1]))
            fill("v2", rw_v2[l - 1])
        fill("uq", two(mla_w_uq[l]))
        kv = mla_w_ukv[l].reshape(P, 4, 2, HD)
        fill("ukv", kv.transpose(0, 2, 1, 3).reshape(P, 512))

    vecs = np.zeros((P, NVEC), np.float32)

    def columns(name, v):
        v = v.reshape(-1, P)
        vecs[:, VEC[name]:VEC[name] + v.shape[0]] = v.T
    for name, v in (("c", c), ("cc", c_ctx), ("b_mod", b_mod), ("norm1", norm1), ("norm2", norm2),
                    ("final", final_norm), ("mu", rw_mu), ("w0", rw_w0), ("a0", rw_a0), ("v0", rw_v0),
                    ("k_k", rw_k_k), ("k_a", rw_k_a), ("r_k", rw_r_k), ("ln_w", rw_ln_w), ("ln_b", rw_ln_b),
                    ("mla_q", mla_q_norm), ("mla_kv", mla_kv_norm), ("ga_q", np.tile(ga_q_norm, (1, 2))),
                    ("ga_k", np.tile(ga_k_norm, (1, 2)))):
        columns(name, v)
    vecs[:, VEC["sink"]:VEC["sink"] + 8] = sw_sink.reshape(1, 8)
    vecs[:, VEC["eps"]], vecs[:, VEC["eps_kk"]], vecs[:, VEC["eps_gn"]] = 1e-6, 1e-12, 64e-5

    tokens = np.concatenate([ctx[0], x[0]], 0)
    xin = np.ascontiguousarray(tokens.reshape(TOK, KD, P).transpose(2, 1, 0))
    router = np.ascontiguousarray(moe_router[0].reshape(KD, P, EXPERTS).transpose(1, 0, 2))
    return stream, small, vecs, router, xin


def constants():
    cn = np.zeros((P, NCN), np.float32)

    def put(name, m):
        cn[:m.shape[0], CN[name]:CN[name] + m.shape[1]] = m
    row, col = np.arange(P)[:, None], np.arange(P)[None, :]
    put("ident", (row == col) * 1.0)
    put("ones", np.ones((P, P)))
    put("heads", (row // HD == col // HD) * 1.0)
    put("tri", (row <= col) * 1.0)
    for name, upper in (("0", True), ("1", False)):
        strict = (row < col) if upper else (row > col)
        near = row // 16 == col // 16
        put("strict" + name, strict * 1.0)
        put("incl" + name, (strict | (row == col)) * 1.0)
        put("near" + name, (strict & near) * 1.0)
        put("far" + name, (strict & ~near) * 1.0)

    def angles(rot):
        r = np.repeat(np.arange(LAT // 64, dtype=np.float32), 64)
        q = np.tile(np.arange(64, dtype=np.float32), LAT // 64)
        nf = rot // 4
        inv = (np.float32(10000.0) ** (-np.arange(nf, dtype=np.float32) / np.float32(nf))).astype(np.float32)
        return np.concatenate([r[:, None] * inv, q[:, None] * inv], 1).T.astype(np.float32)

    def turn(rot):
        h = rot // 2
        m = np.zeros((rot, rot))
        m[np.arange(h) + h, np.arange(h)] = -1
        m[np.arange(h), np.arange(h) + h] = 1
        return m
    a = angles(HD)
    put("cos64", np.tile(np.cos(a), (4, 1)))
    put("sin64", np.tile(np.sin(a), (4, 1)))
    put("rot64", np.kron(np.eye(2), turn(HD)))
    a = angles(32)
    put("cos96", np.concatenate([np.ones((HD, LAT)), np.tile(np.cos(a), (2, 1))]))
    put("sin96", np.concatenate([np.zeros((HD, LAT)), np.tile(np.sin(a), (2, 1))]))
    m = np.zeros((96, 96))
    m[HD:, HD:] = turn(32)
    put("rot96", m)
    q = np.arange(LAT)[:, None]
    k = np.arange(LAT)[None, :]
    band = np.where(np.abs(q - k) <= 128, 0.0, NEG)
    put("band", np.concatenate([band[:P], band[P:]], 1))
    put("iota", np.tile(np.arange(256.0), (P, 1)))
    put("lane8", np.tile(np.arange(8.0), (P, 1)))
    return cn


def kernel(**inputs):
    import concourse.bacc as bacc
    from concourse.bass_utils import run_bass_kernel_spmd as run

    stream, small, vecs, router, xin = layouts(**{k: np.asarray(v) for k, v in inputs.items()})
    arrays = {"wstream": stream, "small": small, "vecs": vecs, "consts": constants(), "router": router, "xin": xin}
    steps = {}
    for _ in range(2):
        nc = bacc.Bacc("TRN2", target_bir_lowering=False, num_devices=1)
        aps = [nc.dram_tensor(k, a.shape, mybir.dt.from_np(a.dtype), kind="ExternalInput").ap()
               for k, a in arrays.items()]
        out = nc.dram_tensor("out", (P, KD, LAT), F32, kind="ExternalOutput").ap()
        steps = backbone(nc, *aps, out, steps)
    r = run(nc, [arrays], core_ids=[0])
    got = np.asarray(r.results[0]["out"])
    return np.ascontiguousarray(got.transpose(2, 1, 0).reshape(1, LAT, D))
```
